# Optimizing a Trainium2 kernel written in Bass

```python
import jax
import jax.numpy as jnp
from jax import lax
import numpy as np
import math

D_MODEL = 1024
BATCH = 1
SEQ = 256
DEPTH = 2

MLSTM_HEADS = 4
MLSTM_DQK = 64
MLSTM_DV = 128
MLSTM_CHUNK = 64
CONV_WIDTH = 4
MOBA_HEADS = 4
MOBA_DH = 64
MOBA_BLOCK = 256
MOBA_TOPK = 3
MOBA_Q_BLOCK = 64
ROPE_THETA = 500000.0
PARTIAL_ROPE_DIM = MOBA_DH // 4
MLA_HEADS = 4
MLA_NOPE = 64
MLA_ROPE = 32
MLA_DV = 64
MLA_Q_LORA = 384
MLA_KV_LORA = 256
MLA_ROPE_THETA = 10000.0
ATTN_Q_BLOCK = 128
D_FF = 4 * D_MODEL
NORM_EPS = 1e-6

MLSTM_WIDTH = MLSTM_HEADS * MLSTM_DV
MOBA_WIDTH = MOBA_HEADS * MOBA_DH
MLA_WIDTH = MLA_HEADS * MLA_DV
MIX_WIDTH = MLSTM_WIDTH + MOBA_WIDTH + MLA_WIDTH
MLA_QK_DIM = MLA_NOPE + MLA_ROPE
IN_SPLITS = (
    2 * MLSTM_HEADS * MLSTM_DQK,
    MLSTM_WIDTH,
    MLSTM_WIDTH,
    MLSTM_HEADS,
    MLSTM_HEADS,
    3 * MOBA_WIDTH,
    MLA_Q_LORA,
    MLA_KV_LORA,
    MLA_ROPE,
)
D_IN = sum(IN_SPLITS)


def rms_norm(x, g):
    xf = x.astype(jnp.float32)
    y = xf * lax.rsqrt(jnp.mean(xf * xf, axis=-1, keepdims=True) + NORM_EPS)
    return (y * g.astype(jnp.float32)).astype(x.dtype)

def rope_tables(positions, dim, theta):
    inv_freq = jnp.power(jnp.float32(theta), -jnp.arange(0, dim, 2, dtype=jnp.float32) / dim)
    ang = positions.astype(jnp.float32)[..., None] * inv_freq
    return jnp.cos(ang), jnp.sin(ang)

def rotate(x, cos, sin):
    half = x.shape[-1] // 2
    x1 = x[..., :half].astype(jnp.float32)
    x2 = x[..., half:].astype(jnp.float32)
    c = cos[:, :, None, :]
    s = sin[:, :, None, :]
    return jnp.concatenate([x1 * c - x2 * s, x2 * c + x1 * s], axis=-1).astype(x.dtype)

def causal_depthwise_conv(x, w, b):
    C = x.shape[-1]
    y = lax.conv_general_dilated(
        x, w[:, None, :].astype(x.dtype), window_strides=(1,),
        padding=[(CONV_WIDTH - 1, 0)], dimension_numbers=('NWC', 'WIO', 'NWC'),
        feature_group_count=C)
    return y + b.astype(x.dtype)

def mlstm_chunkwise(q, k, v, i_pre, f_pre):
    B, S, H, DK = q.shape
    DV = v.shape[-1]
    L = MLSTM_CHUNK
    NC = S // L
    f32 = jnp.float32
    q = q.astype(f32) * (DK ** -0.5)
    k = k.astype(f32)
    v = v.astype(f32)
    log_f = jax.nn.log_sigmoid(f_pre.astype(f32))
    log_i = i_pre.astype(f32)

    def chunks(t):
        return t.reshape((B, NC, L) + t.shape[2:]).swapaxes(0, 1)

    causal = jnp.tril(jnp.ones((L, L), dtype=bool))

    def step(carry, inp):
        C, n, m = carry
        qj, kj, vj, lfj, lij = inp
        bt = jnp.cumsum(lfj, axis=1).transpose(0, 2, 1)
        it = lij.transpose(0, 2, 1)
        log_d = bt[:, :, :, None] - bt[:, :, None, :] + it[:, :, None, :]
        log_d = jnp.where(causal, log_d, -jnp.inf)
        log_inter = bt + m[:, :, None]
        m_t = jnp.maximum(log_inter, jnp.max(log_d, axis=-1))
        d = jnp.exp(log_d - m_t[..., None])
        inter = jnp.exp(log_inter - m_t)
        s = jnp.einsum('blhd,bshd->bhls', qj, kj) * d
        num = (jnp.einsum('bhls,bshv->bhlv', s, vj)
               + inter[..., None] * jnp.einsum('blhd,bhvd->bhlv', qj, C))
        den = jnp.sum(s, axis=-1) + inter * jnp.einsum('blhd,bhd->bhl', qj, n)
        h = num / jnp.maximum(jnp.abs(den), jnp.exp(-m_t))[..., None]
        b_last = bt[:, :, -1]
        log_w = b_last[:, :, None] - bt + it
        m_new = jnp.maximum(b_last + m, jnp.max(log_w, axis=-1))
        w = jnp.exp(log_w - m_new[..., None])
        decay = jnp.exp(b_last + m - m_new)
        C_new = decay[..., None, None] * C + jnp.einsum('bhs,bshv,bshd->bhvd', w, vj, kj)
        n_new = decay[..., None] * n + jnp.einsum('bhs,bshd->bhd', w, kj)
        return (C_new, n_new, m_new), h.transpose(0, 2, 1, 3)

    init = (jnp.zeros((B, H, DV, DK), f32), jnp.zeros((B, H, DK), f32), jnp.zeros((B, H), f32))
    _, h = lax.scan(step, init, (chunks(q), chunks(k), chunks(v), chunks(log_f), chunks(log_i)))
    return h.swapaxes(0, 1).reshape(B, S, H, DV)

def moba_attention(q, k, v):
    B, S, H, D = q.shape
    BS = MOBA_BLOCK
    QB = MOBA_Q_BLOCK
    NB = -(-S // BS)
    S_pad = NB * BS
    K = min(MOBA_TOPK, NB)
    scale = D ** -0.5
    qh = q.transpose(0, 2, 1, 3)
    pad = ((0, 0), (0, 0), (0, S_pad - S), (0, 0))
    kb = jnp.pad(k.transpose(0, 2, 1, 3), pad).reshape(B, H, NB, BS, D)
    vb = jnp.pad(v.transpose(0, 2, 1, 3), pad).reshape(B, H, NB, BS, D)
    k_mean = jnp.mean(kb.astype(jnp.float32), axis=3)
    b_idx = jnp.arange(B)[:, None, None, None]
    h_idx = jnp.arange(H)[None, :, None, None]

    def one_block(qi):
        start = qi * QB
        q_blk = lax.dynamic_slice_in_dim(qh, start, QB, axis=2)
        own = start // BS
        gate = jnp.einsum('bhqd,bhnd->bhqn', q_blk.astype(jnp.float32), k_mean)
        gate = jnp.where(jnp.arange(NB) < own, gate, -jnp.inf)
        _, sel = lax.top_k(gate, K)
        sel_valid = jnp.arange(K) < own
        k_sel = kb[b_idx, h_idx, sel]
        v_sel = vb[b_idx, h_idx, sel]
        s_sel = jnp.einsum('bhqd,bhqkjd->bhqkj', q_blk, k_sel).astype(jnp.float32) * scale
        s_sel = jnp.where(sel_valid[:, None], s_sel, -jnp.inf)
        k_own = lax.dynamic_index_in_dim(kb, own, axis=2, keepdims=False)
        v_own = lax.dynamic_index_in_dim(vb, own, axis=2, keepdims=False)
        s_own = jnp.einsum('bhqd,bhjd->bhqj', q_blk, k_own).astype(jnp.float32) * scale
        q_pos = start + jnp.arange(QB)
        k_pos = own * BS + jnp.arange(BS)
        s_own = jnp.where(k_pos[None, :] <= q_pos[:, None], s_own, -jnp.inf)
        s = jnp.concatenate([s_sel.reshape(B, H, QB, K * BS), s_own], axis=-1)
        p = jax.nn.softmax(s, axis=-1).astype(v.dtype)
        p_sel = p[..., :K * BS].reshape(B, H, QB, K, BS)
        p_own = p[..., K * BS:]
        return (jnp.einsum('bhqkj,bhqkjd->bhqd', p_sel, v_sel)
                + jnp.einsum('bhqj,bhjd->bhqd', p_own, v_own))

    out = lax.map(one_block, jnp.arange(S // QB))
    return out.transpose(1, 0, 3, 2, 4).reshape(B, S, H, D)

def causal_block_attention(q, k, v):
    B, S, H, Dk = q.shape
    Dv = v.shape[-1]
    QB = ATTN_Q_BLOCK
    scale = Dk ** -0.5
    qh = q.transpose(0, 2, 1, 3)
    kh = k.transpose(0, 2, 1, 3)
    vh = v.transpose(0, 2, 1, 3)
    k_pos = jnp.arange(S)

    def one_block(qi):
        start = qi * QB
        q_blk = lax.dynamic_slice_in_dim(qh, start, QB, axis=2)
        s = jnp.einsum('bhqd,bhkd->bhqk', q_blk, kh).astype(jnp.float32) * scale
        q_pos = start + jnp.arange(QB)
        s = jnp.where(k_pos[None, :] <= q_pos[:, None], s, -jnp.inf)
        p = jax.nn.softmax(s, axis=-1).astype(vh.dtype)
        return jnp.einsum('bhqk,bhkd->bhqd', p, vh)

    out = lax.map(one_block, jnp.arange(S // QB))
    return out.transpose(1, 0, 3, 2, 4).reshape(B, S, H, Dv)

def hybrid_layer(x, cos_p, sin_p, cos_d, sin_d, w_in, conv_w, conv_b, b_igate, b_fgate,
                 g_mix_norm, g_mlstm_out, g_moba_q, g_moba_k, g_moba_out, g_cq, g_ckv,
                 w_uq, w_ukv, g_mla_q, g_mla_k, g_mla_out, w_out, g_mlp_norm, w_up, w_down):
    B, S, _ = x.shape
    h = rms_norm(x, g_mix_norm)
    proj = h @ w_in
    offsets = [int(o) for o in np.cumsum(IN_SPLITS)[:-1]]
    m_qk, m_v, m_o, m_i, m_f, moba_qkv, cq, ckv, kpe = jnp.split(proj, offsets, axis=-1)

    qk = jax.nn.silu(causal_depthwise_conv(m_qk, conv_w, conv_b))
    mq, mk = jnp.split(qk, 2, axis=-1)
    mq = mq.reshape(B, S, MLSTM_HEADS, MLSTM_DQK)
    mk = mk.reshape(B, S, MLSTM_HEADS, MLSTM_DQK)
    mv = m_v.reshape(B, S, MLSTM_HEADS, MLSTM_DV)
    hm = mlstm_chunkwise(mq, mk, mv, m_i + b_igate, m_f + b_fgate).astype(x.dtype)
    hm = rms_norm(hm, g_mlstm_out) * jax.nn.sigmoid(m_o).reshape(B, S, MLSTM_HEADS, MLSTM_DV)

    aq, ak, av = jnp.split(moba_qkv.reshape(B, S, 3 * MOBA_HEADS, MOBA_DH), 3, axis=2)
    aq = rms_norm(aq, g_moba_q)
    ak = rms_norm(ak, g_moba_k)
    aq = jnp.concatenate([rotate(aq[..., :PARTIAL_ROPE_DIM], cos_p, sin_p), aq[..., PARTIAL_ROPE_DIM:]], axis=-1)
    ak = jnp.concatenate([rotate(ak[..., :PARTIAL_ROPE_DIM], cos_p, sin_p), ak[..., PARTIAL_ROPE_DIM:]], axis=-1)
    ha = rms_norm(moba_attention(aq, ak, av), g_moba_out)

    lq = (rms_norm(cq, g_cq) @ w_uq).reshape(B, S, MLA_HEADS, MLA_QK_DIM)
    kv = (rms_norm(ckv, g_ckv) @ w_ukv).reshape(B, S, MLA_HEADS, MLA_NOPE + MLA_DV)
    lk = jnp.concatenate(
        [kv[..., :MLA_NOPE], jnp.broadcast_to(kpe[:, :, None, :], (B, S, MLA_HEADS, MLA_ROPE))], axis=-1)
    lv = kv[..., MLA_NOPE:]
    lq = rms_norm(lq, g_mla_q)
    lk = rms_norm(lk, g_mla_k)
    lq = jnp.concatenate([lq[..., :MLA_NOPE], rotate(lq[..., MLA_NOPE:], cos_d, sin_d)], axis=-1)
    lk = jnp.concatenate([lk[..., :MLA_NOPE], rotate(lk[..., MLA_NOPE:], cos_d, sin_d)], axis=-1)
    hl = rms_norm(causal_block_attention(lq, lk, lv), g_mla_out)

    mix = jnp.concatenate([hm.reshape(B, S, MLSTM_WIDTH), ha.reshape(B, S, MOBA_WIDTH),
                           hl.reshape(B, S, MLA_WIDTH)], axis=-1)
    x = x + mix @ w_out

    h2 = rms_norm(x, g_mlp_norm)
    x = x + jnp.square(jax.nn.relu(h2 @ w_up)) @ w_down
    return x

def first_inputs(seed: int = 0) -> dict:
    key = jax.random.key(seed)
    ks = jax.random.split(key, 24)
    f32 = jnp.float32

    def nrm(k, shape, scale):
        return jax.random.normal(k, shape, f32) * scale

    def gain(k, shape):
        return 1.0 + 0.02 * jax.random.normal(k, shape, f32)

    Ld = DEPTH
    x = nrm(ks[0], (BATCH, SEQ, D_MODEL), 1.0)
    offset = jax.random.randint(ks[1], (BATCH, 1), 0, 4096, dtype=jnp.int32)
    positions = offset + jnp.arange(SEQ, dtype=jnp.int32)[None, :]
    return {
        'x': x,
        'positions': positions,
        'w_in': nrm(ks[2], (Ld, D_MODEL, D_IN), D_MODEL ** -0.5),
        'conv_w': nrm(ks[3], (Ld, CONV_WIDTH, 2 * MLSTM_HEADS * MLSTM_DQK), 0.5),
        'conv_b': nrm(ks[4], (Ld, 2 * MLSTM_HEADS * MLSTM_DQK), 0.01),
        'b_igate': nrm(ks[5], (Ld, MLSTM_HEADS), 0.1),
        'b_fgate': 3.0 + nrm(ks[6], (Ld, MLSTM_HEADS), 0.5),
        'g_mix_norm': gain(ks[7], (Ld, D_MODEL)),
        'g_mlstm_out': gain(ks[8], (Ld, MLSTM_HEADS, MLSTM_DV)),
        'g_moba_q': gain(ks[9], (Ld, MOBA_DH)),
        'g_moba_k': gain(ks[10], (Ld, MOBA_DH)),
        'g_moba_out': gain(ks[11], (Ld, MOBA_HEADS, MOBA_DH)),
        'g_cq': gain(ks[12], (Ld, MLA_Q_LORA)),
        'g_ckv': gain(ks[13], (Ld, MLA_KV_LORA)),
        'w_uq': nrm(ks[14], (Ld, MLA_Q_LORA, MLA_HEADS * MLA_QK_DIM), MLA_Q_LORA ** -0.5),
        'w_ukv': nrm(ks[15], (Ld, MLA_KV_LORA, MLA_HEADS * (MLA_NOPE + MLA_DV)), MLA_KV_LORA ** -0.5),
        'g_mla_q': gain(ks[16], (Ld, MLA_QK_DIM)),
        'g_mla_k': gain(ks[17], (Ld, MLA_QK_DIM)),
        'g_mla_out': gain(ks[18], (Ld, MLA_HEADS, MLA_DV)),
        'w_out': nrm(ks[19], (Ld, MIX_WIDTH, D_MODEL), 0.5 * MIX_WIDTH ** -0.5),
        'g_mlp_norm': gain(ks[20], (Ld, D_MODEL)),
        'w_up': nrm(ks[21], (Ld, D_MODEL, D_FF), D_MODEL ** -0.5),
        'w_down': nrm(ks[22], (Ld, D_FF, D_MODEL), 0.5 * D_FF ** -0.5),
    }

def first_block(x, positions, w_in, conv_w, conv_b, b_igate, b_fgate, g_mix_norm, g_mlstm_out,
              g_moba_q, g_moba_k, g_moba_out, g_cq, g_ckv, w_uq, w_ukv, g_mla_q, g_mla_k,
              g_mla_out, w_out, g_mlp_norm, w_up, w_down):
    cos_p, sin_p = rope_tables(positions, PARTIAL_ROPE_DIM, ROPE_THETA)
    cos_d, sin_d = rope_tables(positions, MLA_ROPE, MLA_ROPE_THETA)
    for l in range(DEPTH):
        x = hybrid_layer(
            x, cos_p, sin_p, cos_d, sin_d, w_in[l], conv_w[l], conv_b[l], b_igate[l], b_fgate[l],
            g_mix_norm[l], g_mlstm_out[l], g_moba_q[l], g_moba_k[l], g_moba_out[l], g_cq[l], g_ckv[l],
            w_uq[l], w_ukv[l], g_mla_q[l], g_mla_k[l], g_mla_out[l], w_out[l], g_mlp_norm[l],
            w_up[l], w_down[l])
    return x


A_WIDTH = 512
A_CONV = 3
B_WIDTH = 512
B_CONV = 31
C_HEADS = 8
C_HEAD_DIM = 64
IDX_HEADS = 8
IDX_DIM = 32
TOPK_MAX = 256
DIFF_HEADS = 4
DIFF_HEAD_DIM = 64
NUM_BUCKETS = 32
MAX_DISTANCE = 128
N_ATTN_HEADS = C_HEADS + DIFF_HEADS
N_GROUPS = 4
EXPERTS_PER_GROUP = 8
N_EXPERTS = N_GROUPS * EXPERTS_PER_GROUP
TOP_E = 2
D_EXPERT = 512
Q_BLOCK = 128
MOE_BLOCK = 128
EPS = 1e-6
N_EVEN = (DEPTH + 1) // 2
N_ODD = DEPTH // 2

AB_SIZES = (A_WIDTH, A_WIDTH, A_WIDTH, B_WIDTH, B_WIDTH)
AB_IN = 3 * A_WIDTH + 2 * B_WIDTH
C_WIDTH = C_HEADS * C_HEAD_DIM
DIFF_QK = DIFF_HEADS * 2 * DIFF_HEAD_DIM
DIFF_V = DIFF_HEADS * 2 * DIFF_HEAD_DIM
CD_SIZES = (C_WIDTH, C_WIDTH, C_WIDTH, IDX_HEADS * IDX_DIM, IDX_DIM, IDX_HEADS, DIFF_QK, DIFF_QK, DIFF_V)
CD_IN = 3 * C_WIDTH + IDX_HEADS * IDX_DIM + IDX_DIM + IDX_HEADS + 2 * DIFF_QK + DIFF_V


def rmsnorm(x, g):
    xf = x.astype(jnp.float32)
    y = xf * lax.rsqrt(jnp.mean(xf * xf, axis=-1, keepdims=True) + EPS)
    return (y * g.astype(jnp.float32)).astype(x.dtype)

def layernorm(x, g, b):
    xf = x.astype(jnp.float32)
    mu = jnp.mean(xf, axis=-1, keepdims=True)
    var = jnp.mean(jnp.square(xf - mu), axis=-1, keepdims=True)
    y = (xf - mu) * lax.rsqrt(var + EPS) * g.astype(jnp.float32) + b.astype(jnp.float32)
    return y.astype(x.dtype)

def modulate(h, shift, scale):
    return h * (1 + scale[:, None, :]) + shift[:, None, :]

def split_cols(z, sizes):
    cuts = [int(v) for v in np.cumsum(sizes)[:-1]]
    return jnp.split(z, cuts, axis=-1)

def causal_depthwise_conv_2(u, w):
    width, ch = w.shape
    return lax.conv_general_dilated(u, w[:, None, :].astype(u.dtype), window_strides=(1,),
                                    padding=[(width - 1, 0)],
                                    dimension_numbers=('NWC', 'WIO', 'NWC'),
                                    feature_group_count=ch)

def rel_bucket(dist):
    max_exact = NUM_BUCKETS // 2
    n = jnp.maximum(dist, 0)
    log_ratio = jnp.log(jnp.maximum(n, 1).astype(jnp.float32) / max_exact) / math.log(MAX_DISTANCE / max_exact)
    large = max_exact + (log_ratio * (NUM_BUCKETS - max_exact)).astype(jnp.int32)
    return jnp.where(n < max_exact, n, jnp.minimum(large, NUM_BUCKETS - 1))

def conv_mixers(h, w_in, conv_a, conv_b, conv_b_bias, ln_g, ln_b, w_out):
    gate_b, gate_c, x_a, val_b, glu_gate = split_cols(h @ w_in, AB_SIZES)
    y_a = gate_b * causal_depthwise_conv_2(gate_c * x_a, conv_a)
    u = causal_depthwise_conv_2(val_b * jax.nn.sigmoid(glu_gate), conv_b) + conv_b_bias
    y_b = jax.nn.silu(layernorm(u, ln_g, ln_b))
    return jnp.concatenate([y_a, y_b], axis=-1) @ w_out

def attn_mixers(h, positions, w_in, rel_bias, diff_lam, diff_norm_g, w_out, lambda_init):
    bsz, seq, _ = h.shape
    n_blocks = seq // Q_BLOCK
    topk = min(TOPK_MAX, seq // 4)
    q_c, k_c, v_c, q_idx, k_idx, w_idx, q_d, k_d, v_d = split_cols(h @ w_in, CD_SIZES)
    q_c = q_c.reshape(bsz, seq, C_HEADS, C_HEAD_DIM)
    k_c = k_c.reshape(bsz, seq, C_HEADS, C_HEAD_DIM)
    v_c = v_c.reshape(bsz, seq, C_HEADS, C_HEAD_DIM)
    q_idx = q_idx.reshape(bsz, seq, IDX_HEADS, IDX_DIM)
    q_d = q_d.reshape(bsz, seq, DIFF_HEADS, 2, DIFF_HEAD_DIM)
    k_d = k_d.reshape(bsz, seq, DIFF_HEADS, 2, DIFF_HEAD_DIM)
    q1, q2 = q_d[..., 0, :], q_d[..., 1, :]
    k1, k2 = k_d[..., 0, :], k_d[..., 1, :]
    v_d = v_d.reshape(bsz, seq, DIFF_HEADS, 2 * DIFF_HEAD_DIM)
    lam_f = diff_lam.astype(jnp.float32)
    lam = jnp.exp(jnp.sum(lam_f[0] * lam_f[1])) - jnp.exp(jnp.sum(lam_f[2] * lam_f[3])) + lambda_init
    bias_c = rel_bias[:, :C_HEADS]
    bias_d = rel_bias[:, C_HEADS:]
    scale_c = C_HEAD_DIM ** -0.5
    scale_d = DIFF_HEAD_DIM ** -0.5
    scale_idx = (IDX_DIM * IDX_HEADS) ** -0.5
    gather_rows = jax.vmap(lambda a, i: a[i])

    def block(j):
        s0 = j * Q_BLOCK
        take = lambda a: lax.dynamic_slice_in_dim(a, s0, Q_BLOCK, axis=1)
        pos_q = take(positions)
        causal = positions[:, None, :] <= pos_q[:, :, None]
        rel = jnp.einsum('bqhd,bsd->bqhs', take(q_idx), k_idx)
        score = jnp.einsum('bqhs,bqh->bqs', jax.nn.relu(rel), take(w_idx)).astype(jnp.float32) * scale_idx
        score = jnp.where(causal, score, -jnp.inf)
        _, sel = lax.top_k(score, topk)
        k_sel = gather_rows(k_c, sel)
        v_sel = gather_rows(v_c, sel)
        pos_sel = gather_rows(positions, sel)
        dist_c = pos_q[:, :, None] - pos_sel
        logit_c = (jnp.einsum('bqhd,bqkhd->bhqk', take(q_c), k_sel).astype(jnp.float32) * scale_c
                   + jnp.moveaxis(bias_c[rel_bucket(dist_c)], -1, 1))
        logit_c = jnp.where((dist_c >= 0)[:, None], logit_c, -jnp.inf)
        p_c = jax.nn.softmax(logit_c, axis=-1).astype(v_sel.dtype)
        out_c = jnp.einsum('bhqk,bqkhd->bqhd', p_c, v_sel)
        dist_d = pos_q[:, :, None] - positions[:, None, :]
        b_d = jnp.moveaxis(bias_d[rel_bucket(dist_d)], -1, 1)
        mask_d = causal[:, None]

        def softmax_map(qb, kk):
            lg = jnp.einsum('bqhd,bshd->bhqs', qb, kk).astype(jnp.float32) * scale_d + b_d
            return jax.nn.softmax(jnp.where(mask_d, lg, -jnp.inf), axis=-1)

        attn = softmax_map(take(q1), k1) - lam * softmax_map(take(q2), k2)
        out_d = jnp.einsum('bhqs,bshd->bqhd', attn.astype(v_d.dtype), v_d)
        return out_c, out_d

    out_c, out_d = lax.map(block, jnp.arange(n_blocks))
    out_c = jnp.moveaxis(out_c, 0, 1).reshape(bsz, seq, C_WIDTH)
    out_d = jnp.moveaxis(out_d, 0, 1).reshape(bsz, seq, DIFF_HEADS, 2 * DIFF_HEAD_DIM)
    out_d = (rmsnorm(out_d, diff_norm_g) * (1 - lambda_init)).reshape(bsz, seq, DIFF_V)
    return jnp.concatenate([out_c, out_d], axis=-1) @ w_out

def hier_moe(h, wr_g, br_g, wr_e, br_e, w_gate, w_up, w_down):
    bsz, seq, d = h.shape
    n_tok = bsz * seq
    xf = h.reshape(n_tok, d)
    p_group = jax.nn.softmax((xf @ wr_g + br_g).astype(jnp.float32), axis=-1)
    p_top, g_sel = lax.top_k(p_group, 1)
    fine = (xf @ wr_e + br_e).astype(jnp.float32).reshape(n_tok, N_GROUPS, EXPERTS_PER_GROUP)
    fine = jnp.take_along_axis(fine, g_sel[:, :, None], axis=1)[:, 0]
    e_val, e_sel = lax.top_k(fine, TOP_E)
    gate = (p_top * jax.nn.softmax(e_val, axis=-1)).reshape(-1)
    expert_id = (g_sel * EXPERTS_PER_GROUP + e_sel).reshape(-1)
    token_id = jnp.repeat(jnp.arange(n_tok, dtype=jnp.int32), TOP_E)
    n_assign = n_tok * TOP_E
    order = jnp.argsort(expert_id)
    e_sorted = expert_id[order]
    counts = jnp.bincount(expert_id, length=N_EXPERTS)
    starts = jnp.cumsum(counts) - counts
    padded = (counts + MOE_BLOCK - 1) // MOE_BLOCK * MOE_BLOCK
    pad_end = jnp.cumsum(padded)
    pad_start = pad_end - padded
    dest = pad_start[e_sorted] + jnp.arange(n_assign, dtype=jnp.int32) - starts[e_sorted]
    n_blocks = -(-n_assign // MOE_BLOCK) + N_EXPERTS
    n_rows = n_blocks * MOE_BLOCK
    row_token = jnp.full((n_rows,), n_tok, jnp.int32).at[dest].set(token_id[order])
    row_gate = jnp.zeros((n_rows,), gate.dtype).at[dest].set(gate[order])
    block_expert = jnp.minimum(jnp.searchsorted(pad_end, jnp.arange(n_blocks, dtype=jnp.int32) * MOE_BLOCK, side='right'),
                               N_EXPERTS - 1)
    x_rows = jnp.concatenate([xf, jnp.zeros((1, d), xf.dtype)], axis=0)[row_token].reshape(n_blocks, MOE_BLOCK, d)

    def expert_block(args):
        xb, e = args
        return (jax.nn.silu(xb @ w_gate[e]) * (xb @ w_up[e])) @ w_down[e]

    y_rows = lax.map(expert_block, (x_rows, block_expert)).reshape(n_rows, d)
    y_rows = y_rows * row_gate[:, None].astype(y_rows.dtype)
    out = jnp.zeros((n_tok + 1, d), y_rows.dtype).at[row_token].add(y_rows)[:n_tok]
    return out.reshape(bsz, seq, d)

def second_inputs(seed: int = 0) -> dict:
    key = jax.random.key(seed)
    ks = jax.random.split(key, 32)
    f32 = jnp.float32

    def nrm(k, shape, scale):
        return jax.random.normal(k, shape, f32) * scale

    return {
        'x': nrm(ks[0], (BATCH, SEQ, D_MODEL), 1.0),
        'c': nrm(ks[1], (BATCH, D_MODEL), 1.0),
        'positions': jnp.broadcast_to(jnp.arange(SEQ, dtype=jnp.int32), (BATCH, SEQ)),
        'rel_bias': nrm(ks[2], (NUM_BUCKETS, N_ATTN_HEADS), 0.5),
        'norm_g': 1.0 + nrm(ks[3], (DEPTH, 2, D_MODEL), 0.1),
        'final_norm_g': 1.0 + nrm(ks[4], (D_MODEL,), 0.1),
        'ada_w': nrm(ks[5], (DEPTH, D_MODEL, 6 * D_MODEL), 0.5 * D_MODEL ** -0.5),
        'ada_b': nrm(ks[6], (DEPTH, 6 * D_MODEL), 0.02),
        'ab_w_in': nrm(ks[7], (N_EVEN, D_MODEL, AB_IN), D_MODEL ** -0.5),
        'ab_conv_a': nrm(ks[8], (N_EVEN, A_CONV, A_WIDTH), A_CONV ** -0.5),
        'ab_conv_b': nrm(ks[9], (N_EVEN, B_CONV, B_WIDTH), B_CONV ** -0.5),
        'ab_conv_b_bias': nrm(ks[10], (N_EVEN, B_WIDTH), 0.02),
        'ab_ln_g': 1.0 + nrm(ks[11], (N_EVEN, B_WIDTH), 0.1),
        'ab_ln_b': nrm(ks[12], (N_EVEN, B_WIDTH), 0.02),
        'ab_w_out': nrm(ks[13], (N_EVEN, A_WIDTH + B_WIDTH, D_MODEL), (A_WIDTH + B_WIDTH) ** -0.5),
        'cd_w_in': nrm(ks[14], (N_ODD, D_MODEL, CD_IN), D_MODEL ** -0.5),
        'diff_lam': nrm(ks[15], (N_ODD, 4, DIFF_HEAD_DIM), 0.1),
        'diff_norm_g': 1.0 + nrm(ks[16], (N_ODD, 2 * DIFF_HEAD_DIM), 0.1),
        'cd_w_out': nrm(ks[17], (N_ODD, C_WIDTH + DIFF_V, D_MODEL), (C_WIDTH + DIFF_V) ** -0.5),
        'moe_wr_g': nrm(ks[18], (DEPTH, D_MODEL, N_GROUPS), D_MODEL ** -0.5),
        'moe_br_g': nrm(ks[19], (DEPTH, N_GROUPS), 0.01),
        'moe_wr_e': nrm(ks[20], (DEPTH, D_MODEL, N_EXPERTS), D_MODEL ** -0.5),
        'moe_br_e': nrm(ks[21], (DEPTH, N_EXPERTS), 0.01),
        'moe_w_gate': nrm(ks[22], (DEPTH, N_EXPERTS, D_MODEL, D_EXPERT), D_MODEL ** -0.5),
        'moe_w_up': nrm(ks[23], (DEPTH, N_EXPERTS, D_MODEL, D_EXPERT), D_MODEL ** -0.5),
        'moe_w_down': nrm(ks[24], (DEPTH, N_EXPERTS, D_EXPERT, D_MODEL), D_EXPERT ** -0.5),
    }

def second_block(x, c, positions, rel_bias, norm_g, final_norm_g, ada_w, ada_b,
              ab_w_in, ab_conv_a, ab_conv_b, ab_conv_b_bias, ab_ln_g, ab_ln_b, ab_w_out,
              cd_w_in, diff_lam, diff_norm_g, cd_w_out,
              moe_wr_g, moe_br_g, moe_wr_e, moe_br_e, moe_w_gate, moe_w_up, moe_w_down):
    cond = jax.nn.silu(c)
    for i in range(DEPTH):
        mod = cond @ ada_w[i] + ada_b[i]
        sh1, sc1, g1, sh2, sc2, g2 = jnp.split(mod, 6, axis=-1)
        h = modulate(rmsnorm(x, norm_g[i, 0]), sh1, sc1)
        j = i // 2
        if i % 2 == 0:
            y = conv_mixers(h, ab_w_in[j], ab_conv_a[j], ab_conv_b[j], ab_conv_b_bias[j],
                            ab_ln_g[j], ab_ln_b[j], ab_w_out[j])
        else:
            lambda_init = 0.8 - 0.6 * math.exp(-0.3 * i)
            y = attn_mixers(h, positions, cd_w_in[j], rel_bias, diff_lam[j], diff_norm_g[j],
                            cd_w_out[j], lambda_init)
        x = x + g1[:, None, :] * y
        h = modulate(rmsnorm(x, norm_g[i, 1]), sh2, sc2)
        x = x + g2[:, None, :] * hier_moe(h, moe_wr_g[i], moe_br_g[i], moe_wr_e[i], moe_br_e[i],
                                          moe_w_gate[i], moe_w_up[i], moe_w_down[i])
    return rmsnorm(x, final_norm_g)


def setup_inputs(seed=0):
    out = dict(first_inputs(seed))
    for name, value in second_inputs(seed + 1).items():
        if name != "x":
            out[name + "_2"] = value
    return out


def reference(
    x, positions, w_in, conv_w, conv_b, b_igate, b_fgate, g_mix_norm, g_mlstm_out, g_moba_q,
    g_moba_k, g_moba_out, g_cq, g_ckv, w_uq, w_ukv, g_mla_q, g_mla_k, g_mla_out, w_out,
    g_mlp_norm, w_up, w_down, c_2, positions_2, rel_bias_2, norm_g_2, final_norm_g_2, ada_w_2,
    ada_b_2, ab_w_in_2, ab_conv_a_2, ab_conv_b_2, ab_conv_b_bias_2, ab_ln_g_2, ab_ln_b_2,
    ab_w_out_2, cd_w_in_2, diff_lam_2, diff_norm_g_2, cd_w_out_2, moe_wr_g_2, moe_br_g_2,
    moe_wr_e_2, moe_br_e_2, moe_w_gate_2, moe_w_up_2, moe_w_down_2,
):
    x = first_block(
        x, positions, w_in, conv_w, conv_b, b_igate, b_fgate, g_mix_norm, g_mlstm_out, g_moba_q,
        g_moba_k, g_moba_out, g_cq, g_ckv, w_uq, w_ukv, g_mla_q, g_mla_k, g_mla_out, w_out,
        g_mlp_norm, w_up, w_down,
    )
    return second_block(
        x, c_2, positions_2, rel_bias_2, norm_g_2, final_norm_g_2, ada_w_2, ada_b_2, ab_w_in_2,
        ab_conv_a_2, ab_conv_b_2, ab_conv_b_bias_2, ab_ln_g_2, ab_ln_b_2, ab_w_out_2, cd_w_in_2,
        diff_lam_2, diff_norm_g_2, cd_w_out_2, moe_wr_g_2, moe_br_g_2, moe_wr_e_2, moe_br_e_2,
        moe_w_gate_2, moe_w_up_2, moe_w_down_2,
    )


_drawn_inputs = setup_inputs


def setup_inputs(seed=0):
    import zlib

    import numpy as np

    out = dict(_drawn_inputs(seed))
    spreads = {}
    factors = {'conv_b': 8.0,
     'b_igate': 64.0,
     'g_mix_norm': 2.704,
     'g_mlstm_out': 6.334,
     'g_moba_q': 5.941,
     'g_moba_k': 5.526,
     'g_moba_out': 5.818,
     'g_cq': 5.977,
     'g_ckv': 4.89,
     'g_mla_q': 5.21,
     'g_mla_k': 7.344,
     'g_mla_out': 5.309,
     'g_mlp_norm': 2.908,
     'ab_conv_b_bias_2': 19.157,
     'ab_ln_g_2': 30.289,
     'ab_ln_b_2': 64.0,
     'diff_lam_2': 4.14,
     'diff_norm_g_2': 193.389,
     'moe_br_g_2': 63.632,
     'moe_br_e_2': 64.0,
     'rel_bias_2': 6.165,
     'norm_g_2': 3.954,
     'ada_b_2': 5.875,
     'moe_wr_g_2': 4.009,
     'moe_wr_e_2': 3.972,
     'moe_w_gate_2': 3.697,
     'moe_w_up_2': 3.445,
     'moe_w_down_2': 3.444}
    for name, (base, spread) in spreads.items():
        noise = np.random.default_rng([zlib.crc32(name.encode()), seed]).standard_normal(out[name].shape)
        drawn = base * np.exp(spread * noise) if base else spread * noise
        out[name] = jnp.asarray(drawn.astype(out[name].dtype))
    for name, factor in factors.items():
        out[name] = (out[name] * factor).astype(out[name].dtype)
    return out
```

```python
from contextlib import ExitStack

import numpy as np

import concourse.bass as bass
from concourse import mybir

F32 = mybir.dt.float32
I32 = mybir.dt.int32
ALU = mybir.AluOpType
ACT = mybir.ActivationFunctionType
AX_X = mybir.AxisListType.X

P = 128
S, TT = 256, 2
D, DT = 1024, 8
EPS = 1e-6
NEG = -1e30
SHIFT, M_SHIFT = 0.5, -0.4
L1 = 2
FF = 4096
HM, DQK, DV = 4, 64, 128
C_QK, C_V, C_O, C_IF, C_REST = 0, 512, 1024, 1536, 1544
REST = 1440
CQ, CKV, KPE = 768, 1152, 1408
HA = 4
RING1, UNIT = 5, 4096
U_QK, U_R0, U_R1, U_R2, U_V, U_LORA, U_O, U_OUT, U_MLP = 0, 1, 2, 3, 4, 5, 6, 7, 9
UNITS1 = 25
MLP_ORDER = [("up", 0)] + [x for u in range(1, 8) for x in (("up", u), ("down", u - 1))] + [("down", 7)]

JOBS = (["norm%d" % i for i in range(4)] + ["qk0", "qk1", "gate", "r00", "r01", "r10", "r11", "r20", "r21"]
        + ["aT0", "aT1", "cT0", "cT1", "cT2", "gT", "v0", "v1", "lq0", "lq1", "lkv0", "lkv1", "o0", "o1"]
        + ["lT%d" % i for i in range(4)] + ["mix%d" % i for i in range(4)] + ["post%d" % i for i in range(4)])
JOB = {n: i for i, n in enumerate(JOBS)}
STATS = [("norm", [(0, 2, D)]), ("moba", [(0, 16, 64)]), ("lora", [(0, 2, 384), (2, 2, 256)]), ("mla", [(0, 16, 96)]),
         ("moba_out", [(0, 8, 64)]), ("mlstm_out", [(0, 8, 128)]), ("mla_out", [(0, 8, 64)]), ("post", [(0, 2, D)])]
STAT = {n: i for i, (n, _) in enumerate(STATS)}
R_MIX, R_MLP, R_CW, R_CB, R_GCQ, R_GCKV, R_GOUT, ROWS1 = 0, 8, 16, 32, 36, 39, 41, 49
TWO_PI_A, TWO_PI_B = 6.28125, 0.0019350051879882812
TWO_PI_C = 2 * np.pi - TWO_PI_A - TWO_PI_B
ROUND = 1.5 * 2.0 ** 23

NCH = 7
JOBS2 = (["an%d" % i for i in range(4)] + ["ab%d" % i for i in range(10)] + ["ln_mu", "ln_var"]
         + ["gate0a", "gate0b"] + ["bn%d" % i for i in range(4)]
         + ["cn%d" % i for i in range(4)] + ["gate1a", "gate1b"] + ["qi", "ki"] + ["rel%d" % i for i in range(8)] + ["qc0", "qc1", "kc0", "kc1", "vc0", "vc1"]
         + ["qd0", "qd1", "kd0", "kd1", "vd0", "vd1"]
         + ["oc0", "oc1", "od00", "od01", "od10", "od11"] + ["cm%d" % i for i in range(4)] + ["dn%d" % i for i in range(4)])
JOB2 = {n: i for i, n in enumerate(JOBS2)}
AB_UNITS, AB_OUT, CD_RING, CD_OUT = 5, 5, 4, 7
COLS_OF_CD = [(1536, 296), (0, 512), (512, 512), (1024, 512), (1832, 512), (2344, 512), (2856, 512)]
A_NORM, A_CA, A_BIAS, A_LNG, A_LNB, A_DG, ROWS_A = 0, 32, 44, 48, 52, 56, 57
BUCKETS = 32
THRESHOLDS = [int(np.ceil(16 * 8 ** ((b - 16) / 16) - 1e-9)) for b in range(17, BUCKETS)]
LAMBDA_INIT = 0.8 - 0.6 * float(np.exp(-0.3))
TOPK = 64
L2 = 2
NE, EPG, DE = 32, 8, 512
SLOTS = 64
CHAIN = 400


def spread(ap, dim, n):
    out = ap.unsqueeze(dim)
    return out.broadcast_to([*out.shape[:dim], n, *out.shape[dim + 1:]])


def stand(eng, sem):
    eng.sem_inc(sem, 1)


class Counter:

    def __init__(self, eng, sem):
        self.eng, self.sem, self.base, self.n, self.waited = eng, sem, 0, 0, 0

    def do(self, ins):
        self.n += 1
        return ins.then_inc(self.sem, 1)

    def wait(self):
        if self.n > self.waited:
            self.eng.wait_ge(self.sem, self.base + self.n)
            self.waited = self.n

    def start(self, base):
        self.base, self.n, self.waited = base, 0, 0

    def pad(self):
        self.wait()
        assert self.n <= CHAIN, self.n
        self.eng.sem_inc(self.sem, CHAIN - self.n)


CAUSAL = [[(h, 0, (0,)) for h in range(4)], [(0, 1, (0, 1)), (1, 1, (0, 1))], [(2, 1, (0, 1)), (3, 1, (0, 1))]]
FULL = [[(0, t, (0, 1)), (1, t, (0, 1))] if i == 0 else [(2, t, (0, 1)), (3, t, (0, 1))] for t in range(2) for i in range(2)]
ABANK = [4, 5, 6, 3]
STATS2 = [(2, D), (2, D), (2, D), (8, 128), (2, D), (2, D)]


def first_and_second_block(nc, a, out, stop=None, dbg=None):
    ctx = ExitStack()

    def sb(name, shape, dt=F32):
        return ctx.enter_context(nc.sbuf_tensor(name, shape, dt))

    def sem(name):
        return ctx.enter_context(nc.semaphore(name))

    with ctx:
        bank = ctx.enter_context(nc.psum_tensor("bank", [P, 8, 512], F32))
        ring = sb("ring", [P, 6, UNIT])
        xres = sb("xres", [P, TT, D])
        xn = sb("xn", [P, TT, D])
        hT = sb("hT", [P, DT, S])
        modc = sb("modc", [P, L2, 48])
        ident = sb("ident", [P, P])
        ones = sb("ones", [P, P])
        qmask = sb("qmask", [P, S])
        smask = sb("smask", [P, 3 * P])
        earlier = sb("earlier", [P, P])
        pickh = sb("pickh", [HM, HM, P])
        slot_no = sb("slot_no", [P, SLOTS])
        rowsC = sb("rowsC", [P, P])
        colsC = sb("colsC", [P, P])
        stat = sb("stat", [P, len(STATS), 16])
        rstd = sb("rstd", [P, len(STATS), 16])
        inv_len = sb("inv_len", [P, len(STATS), 16])
        eps16 = sb("eps16", [P, 16])
        sq8 = sb("sq8", [P, 256])
        mhalf = sb("mhalf", [P, 16])
        nmx = sb("nmx", [P, 4, 4])
        esum = sb("esum", [P, TT, 4])
        rsum = sb("rsum", [P, TT, 4])
        cond = sb("cond", [P, DT])
        trig = sb("trig", [P, 8, TT, 24])
        posn = sb("posn", [P, TT])
        posi = sb("posi", [P, TT], I32)
        gbc = sb("gbc", [P, 320])
        bif = sb("bif", [HM, 2])
        WORK = 17024
        work = sb("work", [P, WORK])
        at = [0]

        def take(n, place=None):
            if place is None:
                place = at[0]
                at[0] += n
                assert at[0] <= WORK, at[0]
            return work[:, place:place + n]

        qkv = take(2880).rearrange("p (t n) -> p t n", t=TT)
        og = take(1024).rearrange("p (t n) -> p t n", t=TT)
        tmp = take(1536)
        sc = take(1536).rearrange("p (b n) -> p b n", b=3)
        pT = take(1536).rearrange("p (b n) -> p b n", b=3)
        vext = take(TT * HM * 129).rearrange("p (t h v) -> p t h v", t=TT, h=HM)
        qkpad = take(4 * 259).rearrange("p (c s) -> p c s", c=4)
        qkT = take(1024).rearrange("p (c s) -> p c s", c=4)
        lqk = take(1536).rearrange("p (t h d) -> p t h d", t=TT, h=8)
        lv = take(512).rearrange("p (t h d) -> p t h d", t=TT, h=HA)
        base_l = at[0]
        lT = take(2048).rearrange("p (h s) -> p h s", h=8)
        cv = take(1024, base_l).rearrange("p (c s) -> p c s", c=4)
        cv2 = take(1024, base_l + 1024).rearrange("p (c s) -> p c s", c=4)
        base_a = at[0]
        cT = take(1280).rearrange("p (c s) -> p c s", c=5)
        aT = lT
        crow = work[0:DT, 0:P]
        rows4 = sb("rows4", [HM, 4, S])
        rows = [work[0:HM, 2880 + S * i:2880 + S * i + S] for i in range(4)] + [rows4[:, i, :] for i in range(4)]
        gcol = sb("gcol", [P, 4, HM])
        wgate = sb("wgate", [P, DT, 36])
        uT = work[:, 0:2048].rearrange("p (b c s) -> p b c s", b=2, c=4)
        ru = work[:, 2048:3072].rearrange("p (b n) -> p b n", b=2)
        ada_w = [ring[:, 5, 0:2048].rearrange("p (k n) -> p k n", k=4), ring[:, 5, 2048:4096].rearrange("p (k n) -> p k n", k=4)]
        ada_acc = work[:, 3072:4096].rearrange("p (b n) -> p b n", b=2)
        ada_b = work[0:1, 4096:4096 + 1024].rearrange("p (b n) -> p b n", b=2)
        mT = hT
        NJ = len(JOBS)

        sm = {n: sem(n) for n in (
            "consts", "pool_own", "params_in", "params_first", "cols_ps", "cols_sb", "x_in", "tokens_pos", "trig_dve", "trig_act", "rope_ready", "cond_act",
            "layer_rows_in", "layer_rows_ps", "layer_cols", "layer_small_in", 
            "stat_ready", "rstd_ready", "xn_ready", "job_filled", "job_drained",
            "conv_z", "conv_tanh", "qk_act", "gate_abs", "gate_log", "rows_ready", "rows_exp", "aqk_ready", "lora_ready", "lqk_ready",
            "scores", "masked", "exp_done", "pt_filled", "pt_drained", "pv_done", "o_done",
            "m_bc", "m_arg", "m_exp", "m_s", "m_p", "m_num", "m_h", "o_gate", "mix_ready", "out_filled", "x_done",
            "up_filled", "up_square", "down_done", "ada_acc", "ada_filled", "ada_drained",
            "dve_own", "act_own", "sp_passed", "pe_passed", "stored")}
        ada_in = [sem("ada_in0"), sem("ada_in1")]
        ada_b_in = [sem("ada_b_in0"), sem("ada_b_in1")]
        landed = [sem(f"landed{i}") for i in range(RING1)]
        s = sm

        def B(i):
            return bank[:, i, :]

        w_in = a["w_in"].rearrange("l (k p) n -> l p k n", p=P)
        w_uq = a["w_uq"].rearrange("l (k p) n -> l p k n", p=P)
        w_ukv = a["w_ukv"].rearrange("l (k p) n -> l p k n", p=P)
        w_out = a["w_out"].rearrange("l (u k p) n -> l u p k n", p=P, k=4)
        w_up = a["w_up"].rearrange("l (k p) n -> l p k n", p=P)
        w_down = a["w_down"].rearrange("l (u k p) n -> l u p k n", p=P, k=4)
        ada_src = a["ada_w_2"].rearrange("l (k p) n -> l p k n", p=P)

        ada_bias = a["ada_b_2"].unsqueeze(1)

        def slot(j):
            return ring[:, j % RING1, :]

        def wide(j, n, k=DT):
            return slot(j)[:, 0:k * n].rearrange("p (k n) -> p k n", k=k)

        uq = slot(U_LORA)[:, 0:3 * 384].rearrange("p (k n) -> p k n", k=3)
        ukv = slot(U_LORA)[:, 1152:1152 + 1024].rearrange("p (k n) -> p k n", k=2)

        def moba_q(h):
            return aT[0:64, h, :]

        def moba_k(h):
            return aT[0:64, HA + h, :]

        def moba_v(h, kt):
            return qkv[:, kt, 512 + 64 * h:576 + 64 * h]

        def mla_q(h):
            return lT[0:96, h, :]

        def mla_k(h):
            return lT[0:96, 4 + h, :]

        def mla_v(h, kt):
            return lv[:, kt, h, :]

        def unit_done(l, p):
            first, p = (0, p + UNITS1) if p < 0 else (1, p)
            if p < U_OUT:
                return "job_filled", NJ * l + JOB[{U_QK: "qk1", U_R0: "r01", U_R1: "r11", U_R2: "r21", U_V: "v1", U_LORA: "lkv1", U_O: "o1"}[p]] + 1
            if p < U_MLP:
                return "out_filled", 2 * l + p - U_OUT + 1
            kind, u = MLP_ORDER[p - U_MLP]
            return ("up_filled", 16 * (l + first) + 2 * u + 2) if kind == "up" else ("down_done", 8 * (l + first) + u + 1)

        bias = work[:, 0:6144].rearrange("p (h t n) -> p h t n", h=12, t=TT)
        bkt = work[:, 6144:6656]
        cmask = work[:, 6656:7168].rearrange("p (t n) -> p t n", t=TT)
        rbt = work[:, 7168:7552]
        bno = work[:, 7552:7584]
        colsA = work[:, 7584:7648]
        colsB = work[:, 7648:7776]
        gm = work[:, 7776:7808].rearrange("p (i d) -> p i d", i=4)
        misc = work[:, 7808:8192]
        gbc2 = work[:, 8192:9216]
        ph = 9216

        def region(at, n, **kw):
            assert ph + at + n <= WORK
            return work[:, ph + at:ph + at + n]

        def tiles(ap, c=4):
            return ap.rearrange("p (c s) -> p c s", c=c)

        abx = [tiles(region(1024 * i, 1024)) for i in range(5)]
        pa = tiles(region(5120, 4 * 258))
        pb = tiles(region(6152, 4 * 286))
        mu = region(7296, 256)
        var = region(7552, 256)
        dg_ab3 = region(1024, 1024).rearrange("p (d n) -> p d n", d=DT)
        mixT = xn[:, :, :].rearrange("p t d -> p (t d)").rearrange("p (c s) -> p c s", c=DT)
        rowsA = region(0, 128)
        rowsB = region(128, 128)
        xg = region(0, 1024)
        xeT = region(1024, 1024).rearrange("p (d n) -> p d n", d=DT)
        pick = region(2048, 256).rearrange("p (t n) -> p t n", t=TT)
        pickg = region(2304, 256).rearrange("p (t n) -> p t n", t=TT)
        th = region(2560, 512)
        zz = region(3072, 512)
        aa = region(3584, 512)
        aTe = region(4096, 512).rearrange("p (k n) -> p k n", k=4)
        ye = region(4608, 1024)
        pgT = region(5632, 256)
        wr = region(5888, 288).rearrange("p (k n) -> p k n", k=DT)
        brow = region(6176, 36)
        lg = region(6212, 72).rearrange("p (t n) -> p t n", t=TT)
        rt = [region(6284 + 64 * i, 64).rearrange("p (t n) -> p t n", t=TT) for i in range(9)]
        rk, gg, oh1, oh2, sel_e, fm, fx, fk = rt[:8]
        desc = rt[8]
        rsm = region(6860, 64)
        slotp = region(6924, 64)
        bcmp = region(6988, 32)
        mask_b = region(7020, 512)
        passes_f = region(7532, 8)
        zeros = region(7540, 128)
        mu_var = region(7296, 512)
        od2 = hT[:, 0:4, :].rearrange("p k s -> p (k s)").rearrange("p (t n) -> p t n", t=TT)
        dg_m = region(0, 1024).rearrange("p (d n) -> p d n", d=DT)
        passes_i = [sb("passes0", [1, 1], I32), sb("passes1", [1, 1], I32)]
        sc4 = region(0, 2048).rearrange("p (b n) -> p b n", b=4)
        pT4 = region(2048, 2048).rearrange("p (b n) -> p b n", b=4)
        vcd = region(4096, 2048).rearrange("p (i t n) -> p i t n", i=2, t=TT)
        isc = region(6144, 512).rearrange("p (t n) -> p t n", t=TT)
        iwk = region(6656, 512).rearrange("p (t n) -> p t n", t=TT)
        kiT = region(7168, 256)
        wix = region(7424, 16).rearrange("p (t h) -> p t h", t=TT)
        top8 = region(7440, 16).rearrange("p (t n) -> p t n", t=TT)
        lam_r = misc[:, 0:256]
        lam = misc[:, 256:264]
        dcol = misc[:, 264:265]
        half_cols = misc[:, 265:273]
        orec = misc[:, 280:296]
        lnsq = misc[:, 300:301]
        qiT = region(2048, 2048).rearrange("p (h s) -> p h s", h=8)
        qkC = ring[:, 4, :].rearrange("p (h s) -> p h s", h=16)
        qkD = ring[:, 5, :].rearrange("p (h s) -> p h s", h=16)
        fin_g = region(0, 1024)
        out_sb = xn
        posr = gbc2[:, 256:512]
        posq = misc[:, 370:372]
        with_i = gbc2[:, 0:256]

        s2 = {n: sem(n + "_2") for n in (
            "rows_in", "rows_ps", "cols_done", "small_in", "cols_ready", "pos_ready", "job_filled", "job_drained", "xn_ready", "stat_ready", "rstd_ready", "diag_ready", "gate_row_filled", "gate_row_drained",
            "pa_ready", "u_ready", "uc_ready", "var_ready", "var_sqrt", "zb_ready", "zb_tanh", "yb_ready", "ya_ready", "out_filled", "x_done",
            "rel_used", "scores", "masked", "exp_done", "pt_filled", "pt_drained", "sel_ready", "lam_ready", "lam_exp", "o_ready", "final_in", "moe_small_in")}
        landed2 = [sem(f"landed2_{i}") for i in range(6)]
        landed3 = [sem(f"landed3_{i}") for i in range(CD_RING)]
        sM = {n: sem(f"{n}_m") for n in (
            "logits_ps", "exp_in", "exp_out", "sel_ready", "rank_ps", "passes_ready", "zero_ready", "own_loop", "p_ready", "gathered", "xg_drained", "xt_filled",
            "xt_drained_v", "xt_drained_s", "g_filled", "u_filled", "tanh_done", "g_free", "a_ready", "at_filled", "at_drained",
            "pg_filled", "pg_drained", "y_filled", "y_drained", "scattered", "acc_done")}
        landedM = [sem(f"landed_m{j}") for j in range(6)]
        moe_w = [a[n].rearrange("l e (k p) n -> l e p k n", p=P) for n in ("moe_w_gate_2", "moe_w_up_2")] + [
            a["moe_w_down_2"].rearrange("l e (k p) n -> l e p k n", p=P)]
        MCHAIN = 80
        PAIRS = NE // 2

        def wide2(j, n, k=DT, slots=6):
            return ring[:, j % slots, 0:k * n].rearrange("p (k n) -> p k n", k=k)

        block = ctx.enter_context(nc.Block())

        @block.sync
        def _(sp):
            sp.dma_start(xres[:, :, :], a["x"].rearrange("a (t p) d -> p (a t) d", p=P)).then_inc(s["x_in"], 16)
            sp.sem_inc(s["x_done"], 2)
            sp.dma_start(crow[:, :], a["c_2"].rearrange("a (r p) -> (a r) p", p=P)).then_inc(s["params_first"], 16)
            with nc.allow_non_contiguous_dma("positions and gates, once"):
                sp.dma_start(posi[:, :], a["positions"].rearrange("a (t p) -> p (a t)", p=P)).then_inc(s["tokens_pos"], 16)
            sp.wait_ge(s["consts"], 1)
            with sp.Fori(0, L1) as l:
                sp.wait_ge(s["x_done"], 2 * l + 1)
                stand(sp, s["sp_passed"])
                for r, n, src in ((R_MIX, 8, a["g_mix_norm"].rearrange("l (r p) -> l r p", p=P)),
                                  (R_MLP, 8, a["g_mlp_norm"].rearrange("l (r p) -> l r p", p=P)),
                                  (R_CW, 16, a["conv_w"].rearrange("l w (r p) -> l (w r) p", p=P)),
                                  (R_CB, 4, a["conv_b"].rearrange("l (r p) -> l r p", p=P)),
                                  (R_GCQ, 3, a["g_cq"].rearrange("l (r p) -> l r p", p=P)),
                                  (R_GCKV, 2, a["g_ckv"].rearrange("l (r p) -> l r p", p=P)),
                                  (R_GOUT, 4, a["g_mlstm_out"]),
                                  (R_GOUT + 4, 2, a["g_moba_out"].rearrange("l (r a) d -> l r (a d)", a=2)),
                                  (R_GOUT + 6, 2, a["g_mla_out"].rearrange("l (r a) d -> l r (a d)", a=2))):
                    sp.dma_start(rowsC[r:r + n, :], src[l]).then_inc(s["layer_rows_in"], 16)
                with nc.allow_non_contiguous_dma("small vectors"):
                    for c, n, name in ((0, 64, "g_moba_q"), (64, 64, "g_moba_k"), (128, 96, "g_mla_q"), (224, 96, "g_mla_k")):
                        sp.dma_start(gbc[:, c:c + n], a[name].unsqueeze(1)[l].broadcast_to([P, n])).then_inc(s["layer_small_in"], 16)
                    for c, name in ((0, "b_igate"), (1, "b_fgate")):
                        sp.dma_start(bif[:, c:c + 1], a[name].unsqueeze(2)[l]).then_inc(s["layer_small_in"], 16)
                    for g in range(2):
                        sp.dma_start(wgate[:, :, 32 * g:32 * g + 4], w_in[l, :, :, C_IF + 4 * g:C_IF + 4 * g + 4]).then_inc(s["layer_small_in"], 16)
                loads = [(wide(U_QK, 512), w_in[l, :, :, 0:512])]
                loads += [(wide(U_R0, 512), w_in[l, :, :, C_REST:C_REST + 512]), (wide(U_R1, 512), w_in[l, :, :, C_REST + 512:C_REST + 1024]),
                          (wide(U_R2, 416), w_in[l, :, :, C_REST + 1024:C_REST + REST])]
                loads += [(wide(U_V, 512), w_in[l, :, :, C_V:C_V + 512]), None, (wide(U_O, 512), w_in[l, :, :, C_O:C_O + 512])]
                loads += [(wide(U_OUT + u, 1024, 4), w_out[l, u]) for u in range(2)]
                for i, (kind, u) in enumerate(MLP_ORDER):
                    loads.append((wide(U_MLP + i, 512), w_up[l, :, :, 512 * u:512 * u + 512]) if kind == "up" else
                                 (wide(U_MLP + i, 1024, 4), w_down[l, u]))
                for j in range(UNITS1):
                    kind, value = unit_done(l, j - RING1)
                    sp.wait_ge(s[kind], value)
                    stand(sp, s["sp_passed"])
                    if j == U_LORA:
                        sp.dma_start(uq, w_uq[l]).then_inc(landed[j % RING1], 16)
                        sp.dma_start(ukv, w_ukv[l]).then_inc(landed[j % RING1], 16)
                    else:
                        sp.dma_start(loads[j][0], loads[j][1]).then_inc(landed[j % RING1], 16)
            with nc.allow_non_contiguous_dma("small vectors, once"):
                sp.wait_ge(s["x_done"], 5)
                for r, n, src in ((A_NORM, 32, a["norm_g_2"].rearrange("l i (r p) -> (l i r) p", p=P)),
                                  (A_CA, 12, a["ab_conv_a_2"].rearrange("l w (r p) -> (l w r) p", p=P)),
                                  (A_BIAS, 4, a["ab_conv_b_bias_2"].rearrange("l (r p) -> (l r) p", p=P)),
                                  (A_LNG, 4, a["ab_ln_g_2"].rearrange("l (r p) -> (l r) p", p=P)),
                                  (A_LNB, 4, a["ab_ln_b_2"].rearrange("l (r p) -> (l r) p", p=P)),
                                  (A_DG, 1, a["diff_norm_g_2"])):
                    sp.dma_start(rowsA[r:r + n, :], src).then_inc(s2["rows_in"], 16)
                sp.dma_start(rowsB[0:124, :], a["ab_conv_b_2"].rearrange("l w (r p) -> (l w r) p", p=P)).then_inc(s2["rows_in"], 16)
                sp.dma_start(rbt, a["rel_bias_2"].rearrange("b h -> (b h)").unsqueeze(0).broadcast_to([P, 384])).then_inc(s2["small_in"], 16)
                sp.dma_start(lam_r, a["diff_lam_2"].rearrange("l i d -> l (i d)").broadcast_to([P, 256])).then_inc(s2["small_in"], 16)
                sp.dma_start(with_i.bitcast(I32), a["positions_2"].broadcast_to([P, S])).then_inc(s2["small_in"], 16)
                sp.dma_start(posi[:, :], a["positions_2"].rearrange("a (t p) -> p (a t)", p=P)).then_inc(s2["small_in"], 16)
            ab_in = a["ab_w_in_2"].rearrange("l (k p) n -> p (l k) n", p=P)
            ab_out = a["ab_w_out_2"].rearrange("l (u k p) n -> u p (l k) n", p=P, k=4)
            for j in range(7):
                if j < RING1:
                    kind, value = unit_done(L1, j - RING1)
                    sp.wait_ge(s[kind], value)
                elif j == RING1:
                    sp.wait_ge(s["ada_acc"], 24 * L1 + 2)
                else:
                    sp.wait_ge(s2["job_filled"], JOB2["ab1"] + 1)
                if j < AB_UNITS:
                    sp.dma_start(wide2(j, 512), ab_in[:, :, 512 * j:512 * j + 512]).then_inc(landed2[j % 6], 16)
                else:
                    sp.dma_start(wide2(j, 1024, 4), ab_out[j - AB_OUT]).then_inc(landed2[j % 6], 16)

            def moe_load(i, e, kind, slot):
                if kind == 2:
                    dst = ring[:, slot, :].rearrange("p (k n) -> p k n", k=4)
                else:
                    dst = ring[:, slot, :].rearrange("p (k n) -> p k n", k=DT)
                sp.dma_start(dst, moe_w[kind][i, e]).then_inc(landedM[slot], 16)

            def moe_pairs(i, it0, first):
                m = sM
                with sp.Fori(first, PAIRS) as pr:
                    it = it0 + pr
                    for kind, (name, value) in enumerate((("g_filled", it + 1), ("u_filled", it + 1), ("y_filled", 2 * it + 2))):
                        sp.wait_ge(m[name], value)
                        stand(sp, s["sp_passed"])
                        for e in range(2):
                            moe_load(i, 2 * pr + e, kind, 3 * e + kind)

            def moe_first(i, slots):
                for slot in slots:
                    moe_load(i, slot // 3, slot % 3, slot)

            def moe_stream(i, before):
                m = sM
                moe_pairs(i, before * PAIRS, 1)
                sp.wait_ge(m["passes_ready"], i + 1)
                n = sp.value_load(passes_i[i][0:1, 0:1], min_val=1, max_val=4)
                with sp.If(n > 1):
                    with sp.Fori(1, n) as q:
                        moe_pairs(i, (q + before) * PAIRS, 0)
                return n

            def moe_small(i):
                with nc.allow_non_contiguous_dma("the router, once a layer"):
                    sp.dma_start(wr[:, :, 0:4], a["moe_wr_g_2"].rearrange("l (k p) n -> l p k n", p=P)[i]).then_inc(s2["moe_small_in"], 16)
                    sp.dma_start(wr[:, :, 4:36], a["moe_wr_e_2"].rearrange("l (k p) n -> l p k n", p=P)[i]).then_inc(s2["moe_small_in"], 16)
                    sp.dma_start(brow[:, 0:4], a["moe_br_g_2"][i:i + 1, :].broadcast_to([P, 4])).then_inc(s2["moe_small_in"], 16)
                    sp.dma_start(brow[:, 4:36], a["moe_br_e_2"][i:i + 1, :].broadcast_to([P, 32])).then_inc(s2["moe_small_in"], 16)

            sp.wait_ge(s2["job_filled"], JOB2["ab9"] + 1)
            moe_first(0, (3, 1, 4, 2))
            sp.wait_ge(s2["out_filled"], 2)
            moe_first(0, (0, 5))
            sp.wait_ge(s2["x_done"], 1)
            moe_small(0)
            n0 = moe_stream(0, 0)
            cd_in = a["cd_w_in_2"].rearrange("l (k p) n -> p (l k) n", p=P)
            cd_out = a["cd_w_out_2"].rearrange("l (u k p) n -> u p (l k) n", p=P, k=4)
            last_job = ["ki", "qc1", "kc1", "vc1", "qd1", "kd1", "vd1"]
            for j in range(9):
                if j >= CD_RING:
                    sp.wait_ge(s2["job_filled"], JOB2[last_job[j - CD_RING]] + 1)
                else:
                    name, value = (("g_filled", 1), ("u_filled", 1), ("y_filled", 2), ("g_filled", 1))[j]
                    sp.wait_ge(sM[name], value * PAIRS * n0 + value)
                    stand(sp, s["sp_passed"])
                if j < CD_OUT:
                    c, n = COLS_OF_CD[j]
                    sp.dma_start(wide2(j, n, DT, CD_RING), cd_in[:, :, c:c + n]).then_inc(landed3[j % CD_RING], 16)
                else:
                    sp.dma_start(wide2(j, 1024, 4, CD_RING), cd_out[j - CD_OUT]).then_inc(landed3[j % CD_RING], 16)
            sp.wait_ge(s2["job_filled"], JOB2["vd1"] + 1)
            moe_first(1, (1, 2))
            sp.wait_ge(s2["scores"], 16)
            moe_first(1, (4, 5))
            sp.wait_ge(s2["out_filled"], 4)
            moe_first(1, (3, 0))
            sp.wait_ge(s2["x_done"], 3)
            moe_small(1)
            moe_stream(1, n0)
            sp.wait_ge(sM["acc_done"], 2)
            sp.dma_start(fin_g, a["final_norm_g_2"].unsqueeze(0).broadcast_to([P, D])).then_inc(s2["final_in"], 16)
            sp.wait_ge(s2["o_ready"], 1)
            sp.dma_start(out.rearrange("a (t p) d -> p (a t) d", p=P), out_sb[:, :, :]).then_inc(s["stored"], 16)
            sp.wait_ge(s["stored"], 16)

        @block.gpsimd
        def _(pool):
            own = Counter(pool, s["pool_own"])
            own.do(pool.memset(ident[:, :], 0.0))
            own.do(pool.memset(ones[:, :], 1.0))
            own.do(pool.memset(qmask[:, :], 0.0))
            own.do(pool.memset(smask[:, :], M_SHIFT))
            own.do(pool.memset(earlier[:, :], 1.0))
            own.do(pool.memset(pickh[:, :, :], 1.0))
            own.do(pool.memset(mhalf[:, :], -0.5))
            own.do(pool.memset(eps16[:, :], EPS))
            for i, (_, parts) in enumerate(STATS):
                for c, n, width in parts:
                    own.do(pool.memset(inv_len[:, i, c:c + n], 1.0 / width))
            own.do(pool.memset(wgate[:, :, :], 0.0))
            own.do(pool.memset(qkpad[:, :, 0:3], 0.0))
            own.do(pool.memset(vext[:, :, :, 128:129], 1.0))
            own.do(pool.memset(rowsC[:, :], 0.0))
            own.do(pool.memset(rows4[:, 3, :], 0.0))
            for j in range(24):
                dim, th, jj = (16, 500000.0, j) if j < 8 else (32, 10000.0, j - 8)
                own.do(pool.memset(trig[:, 0, :, j:j + 1], float(np.float32(th ** (-2.0 * jj / dim)))))
            own.wait()
            own.do(pool.affine_select(out=ident[:, :], in_=ident[:, :], compare_op=ALU.not_equal, fill=1.0, base=0,
                                      pattern=[[-1, P]], channel_multiplier=1))
            own.do(pool.affine_select(out=qmask[:, P:S], in_=qmask[:, P:S], compare_op=ALU.is_ge, fill=NEG, base=0,
                                      pattern=[[-1, P]], channel_multiplier=1))
            for c in (0, 2):
                own.do(pool.affine_select(out=smask[:, c * P:c * P + P], in_=smask[:, c * P:c * P + P], compare_op=ALU.is_ge, fill=NEG,
                                          base=0, pattern=[[1, P]], channel_multiplier=-1))
            own.do(pool.affine_select(out=earlier[:, :], in_=earlier[:, :], compare_op=ALU.is_gt, fill=0.0, base=0,
                                      pattern=[[1, P]], channel_multiplier=-1))
            own.do(pool.affine_select(out=pickh[:, :, :], in_=pickh[:, :, :], compare_op=ALU.is_equal, fill=0.0, base=0,
                                      pattern=[[-1, HM], [0, P]], channel_multiplier=1))
            own.do(pool.iota(slot_no[:, :], pattern=[[1, SLOTS]], base=0, channel_multiplier=0, allow_small_or_imprecise_dtypes=True))
            own.wait()
            pool.sem_inc(s["consts"], 1)
            pool.sem_inc(s["ada_acc"], 2)
            pool.sem_inc(s["ada_drained"], 2)
            base = own.n

            def power(l, name):
                i = STAT[name]
                parts = STATS[i][1]
                cols = sum(n for _, n, _ in parts)
                pool.wait_ge(s["stat_ready"], len(STATS) * l + i + 1)
                own.do(pool.tensor_tensor(stat[:, i, 0:cols], stat[:, i, 0:cols], inv_len[:, i, 0:cols], ALU.mult))
                own.wait()
                own.do(pool.tensor_tensor(stat[:, i, 0:cols], stat[:, i, 0:cols], eps16[:, 0:cols], ALU.add))
                own.wait()
                pool.tensor_tensor(rstd[:, i, 0:cols], stat[:, i, 0:cols], mhalf[:, 0:cols], ALU.pow).then_inc(s["rstd_ready"], 1)

            with pool.Fori(0, L1) as l:
                own.start(base + l * CHAIN)
                for name, _ in STATS:
                    power(l, name)
                for c in range(12):
                    for hf in range(2):
                        pool.wait_ge(s["ada_acc"], 24 * l + 2 * c + hf + 1)
                        pool.dma_start(ada_w[hf], ada_src[l, :, 4 * hf:4 * hf + 4, 512 * c:512 * c + 512]).then_inc(ada_in[hf], 16)
                    pool.wait_ge(s["ada_drained"], 12 * l + c + 1)
                    pool.dma_start(ada_b[:, c % 2, :], ada_bias[l, :, 512 * c:512 * c + 512]).then_inc(ada_b_in[c % 2], 16)
                own.pad()


            own.start(base + L1 * CHAIN)
            pool.wait_ge(s["x_done"], 5)
            own.do(pool.iota(bno, pattern=[[1, BUCKETS]], base=0, channel_multiplier=0, allow_small_or_imprecise_dtypes=True))
            own.do(pool.memset(pa[:, :, 0:2], 0.0))
            own.do(pool.memset(pb[:, :, 0:30], 0.0))
            own.wait()
            pool.sem_inc(s2["pos_ready"], 1)

            def power2(n, cols, width):
                i = n % len(STATS)
                pool.wait_ge(s2["stat_ready"], n + 1)
                own.do(pool.tensor_scalar(stat[:, i, 0:cols], stat[:, i, 0:cols], 1.0 / width, EPS, ALU.mult, ALU.add))
                own.wait()
                pool.tensor_tensor(rstd[:, i, 0:cols], stat[:, i, 0:cols], mhalf[:, 0:cols], ALU.pow).then_inc(s2["rstd_ready"], 1)

            for n, (cols, width) in enumerate(STATS2):
                power2(n, cols, width)

        @block.tensor
        def _(pe):
            def job(l, name):
                i = JOB[name]
                if i >= 4:
                    pe.wait_ge(s["job_drained"], NJ * l + i - 3)
                return B(i % 4)

            def filled(ins):
                ins.then_inc(s["job_filled"], 1)

            def unit(l, j):
                n = (2 if j == U_LORA else 1)
                per = UNITS1 // RING1 + (1 if j % RING1 == U_LORA % RING1 else 0)
                k = j // RING1 + (1 if j % RING1 == U_LORA % RING1 and j >= U_LORA else 0) + 1
                pe.wait_ge(landed[j % RING1], 16 * per * l + 16 * k)

            def transposes(l, names, src, dst_cols):
                for i, nm in enumerate(names):
                    b = job(l, nm)
                    for c in range(2 * i, 2 * i + 2):
                        for t in range(TT):
                            if c < dst_cols:
                                ap = src(c, t)
                                last = pe.transpose(b[0:ap.shape[1], (c % 2) * S + t * P:(c % 2) * S + t * P + P], ap, ident[:, :])
                    filled(last)

            def natural(l, name, t, w, n, kk=DT, x=None):
                b = job(l, name)
                for k in reversed(range(kk)):
                    last = pe.matmul(b[:, 0:n], (hT if x is None else x)[:, k, t * P:t * P + P], w[:, k, 0:n], start=(k == kk - 1), stop=(k == 0))
                return last

            def scores(g, q, kf, plan, after=()):
                for i, heads in enumerate(plan):
                    col = 0
                    for h, t, kts in heads:
                        for kt in kts:
                            pass
                        n = P * len(kts)
                        last = pe.matmul(B(ABANK[i])[:, col:col + n], q(h)[:, t * P:t * P + P], kf(h)[:, 0:n], start=True, stop=True)
                        col += n
                    last.then_inc(s["scores"], 1)

            def p_transposes(g0, plan):
                for i, heads in enumerate(plan):
                    pe.wait_ge(s["exp_done"], g0 + i + 1)
                    for c in range(4):
                        last = pe.transpose(B(ABANK[i])[:, c * P:c * P + P], sc[:, i, c * P:c * P + P], ident[:, :])
                    last.then_inc(s["pt_filled"], 1)

            def values(g0, plan, v, out_of):
                pe.wait_ge(s["pt_drained"], g0 + len(plan))
                for i, heads in enumerate(plan):
                    c = 0
                    for h, t, kts in heads:
                        for kt in kts:
                            last = pe.matmul(out_of(t, h), pT[:, i, c * P:c * P + P], v(h, kt), start=(kt == kts[0]), stop=(kt == kts[-1]))
                            c += 1
                last.then_inc(s["pv_done"], 1)

            def o64(t, h):
                return B(7)[:, 256 * t + 64 * h:256 * t + 64 * h + 64]

            def mlp_up(l, i, u):
                unit(l, U_MLP + i)
                w = wide(U_MLP + i, 512)
                for b in range(2):
                    pe.wait_ge(s["up_square"], 16 * l + 2 * u + b + 1)
                    for c in range(2 * b, 2 * b + 2):
                        for k in range(DT):
                            last = pe.matmul(B(4 + b)[:, (c % 2) * S:(c % 2) * S + S], w[:, k, c * P:c * P + P], hT[:, k, :],
                                             start=(k == 0), stop=(k == DT - 1))
                    if b == 0:
                        last.then_inc(s["up_filled"], 1)
                last.then_inc(s["up_filled"], 1)

            def mlp_down(l, i, u):
                unit(l, U_MLP + i)
                pe.wait_ge(s["up_square"], 16 * l + 2 * u + 4)
                w = wide(U_MLP + i, 1024, 4)
                for t in range(TT):
                    for hf in range(2):
                        for k in range(4):
                            last = pe.matmul(B(2 * t + hf), uT[:, u % 2, k, t * P:t * P + P], w[:, k, 512 * hf:512 * hf + 512],
                                             start=(u == 0 and k == 0), stop=(u == 7 and k == 3), skip_group_check=True)
                last.then_inc(s["down_done"], 1)

            def ada_sum(l, c):
                pe.wait_ge(s["ada_acc"], 24 * l + 2 * c + 4)
                pe.wait_ge(ada_b_in[c % 2], 96 * l + 16 * (c // 2 + 1))
                pe.wait_ge(s["ada_drained"], 12 * l + c + 2)
                for j in range(4):
                    pe.matmul(B(6)[:, j:j + 1], ada_acc[:, c % 2, j * P:j * P + P], ones[:, 0:1], start=True, stop=False)
                    last = pe.matmul(B(6)[:, j:j + 1], ada_b[:, c % 2, j * P:j * P + P], ones[0:1, 0:1], start=False, stop=True)
                last.then_inc(s["ada_filled"], 1)

            pe.sem_inc(s["up_filled"], 16)
            pe.sem_inc(s["down_done"], 8)
            pe.wait_ge(s["consts"], 1)
            pe.wait_ge(s["params_first"], 16)
            pe.transpose(B(4)[:, 0:DT], crow[:, :], ident[0:DT, 0:DT]).then_inc(s["cols_ps"], 1)

            with pe.Fori(0, L1) as l:
                pe.wait_ge(s["layer_rows_in"], 144 * l + 144)
                pe.wait_ge(s["layer_small_in"], 128 * l + 128)
                pe.wait_ge(s["cols_sb"], 1)
                pe.transpose(B(5)[:, 0:P], rowsC[:, :], ident[:, :]).then_inc(s["layer_rows_ps"], 1)
                for t in range(TT):
                    pe.wait_ge(s["xn_ready"], 4 * l + t + 1)
                transposes(l, ["norm%d" % i for i in range(4)], lambda c, t: xn[:, t, c * P:c * P + P], DT)
                pe.wait_ge(s["job_drained"], NJ * l + JOB["norm3"] + 1)
                unit(l, U_QK)
                w = wide(U_QK, 512)
                for i in range(2):
                    b = job(l, "qk%d" % i)
                    for c in range(2 * i, 2 * i + 2):
                        for k in range(DT):
                            last = pe.matmul(b[:, (c % 2) * S:(c % 2) * S + S], w[:, k, c * P:c * P + P], hT[:, k, :], start=(k == 0), stop=(k == DT - 1))
                    if i == 0:
                        filled(last)
                filled(last)
                b = job(l, "gate")
                for k in range(DT):
                    last = pe.matmul(b[0:36, 0:S], wgate[:, k, :], hT[:, k, :], start=(k == 0), stop=(k == DT - 1))
                filled(last)
                for u, n, nm in ((U_R0, 512, "r0"), (U_R1, 512, "r1"), (U_R2, 416, "r2")):
                    unit(l, u)
                    for t in range(TT):
                        filled(natural(l, nm + str(t), t, wide(u, n), n))
                pe.wait_ge(s["aqk_ready"], l + 1)
                transposes(l, ["aT0", "aT1"], lambda c, t: qkv[:, t, c * P:c * P + P], 4)
                pe.wait_ge(s["lora_ready"], l + 1)
                transposes(l, ["cT0", "cT1", "cT2"], lambda c, t: qkv[:, t, CQ + c * P:CQ + c * P + P], 5)
                pe.wait_ge(s["job_drained"], NJ * l + JOB["aT1"] + 1)
                scores(None, moba_q, moba_k, CAUSAL)
                pe.wait_ge(s["rows_exp"], l + 1)
                b = job(l, "gT")
                stand(pe, s["pe_passed"])
                for q in range(2):
                    for t in range(TT):
                        last = pe.transpose(b[:, 4 * (2 * q + t):4 * (2 * q + t) + 4], rows[5 + q][:, t * P:t * P + P], ident[0:HM, 0:HM])
                filled(last)
                unit(l, U_V)
                for t in range(TT):
                    filled(natural(l, "v%d" % t, t, wide(U_V, 512), 512))
                p_transposes(6 * l, CAUSAL)
                unit(l, U_LORA)
                for t in range(TT):
                    filled(natural(l, "lq%d" % t, t, uq, 384, 3, cT))
                for t in range(TT):
                    filled(natural(l, "lkv%d" % t, t, ukv, 512, 2, cT[:, 3:5, :]))
                values(6 * l, CAUSAL, moba_v, o64)
                unit(l, U_O)
                for t in range(TT):
                    filled(natural(l, "o%d" % t, t, wide(U_O, 512), 512))
                pe.wait_ge(s["lqk_ready"], l + 1)
                transposes(l, ["lT%d" % i for i in range(4)], lambda c, t: lqk[:, t, c, :], 8)
                pe.wait_ge(s["rows_ready"], l + 1)
                pe.wait_ge(s["o_done"], 2 * l + 1)
                for h in range(HM):
                    last = pe.matmul(B(6 + h // 2)[:, (h % 2) * S:(h % 2) * S + S], pickh[:, h, :], rows[4], start=True, stop=True)
                    if h % 2:
                        last.then_inc(s["m_bc"], 1)
                pe.wait_ge(s["qk_act"], l + 1)
                for h0 in (0, 2):
                    for h in (h0, h0 + 1):
                        if h0:
                            pe.wait_ge(s["m_h"], 4 * l + h - 1)
                        q = qkT[64 * (h % 2):64 * (h % 2) + 64, h // 2, :]
                        k = qkT[64 * (h % 2):64 * (h % 2) + 64, 2 + h // 2, :]
                        pe.matmul(B(4 + h % 2)[:, 0:S], k[:, 0:P], q, start=True, stop=True)
                        pe.matmul(B(4 + h % 2)[:, S:3 * P], k[:, P:S], q[:, P:S], start=True, stop=True).then_inc(s["m_s"], 1)
                    for h in (h0, h0 + 1):
                        pe.wait_ge(s["m_p"], 4 * l + h + 1)
                        pm = pT[:, h % 2, :]
                        b = B(4 + h % 2)
                        pe.matmul(b[:, 0:129], pm[:, 0:P], vext[:, 0, h, :], start=True, stop=True)
                        pe.matmul(b[:, 129:258], pm[:, P:S], vext[:, 0, h, :], start=True, stop=False)
                        pe.matmul(b[:, 129:258], pm[:, S:3 * P], vext[:, 1, h, :], start=False, stop=True).then_inc(s["m_num"], 1)
                pe.wait_ge(s["m_h"], 4 * l + 4)
                pe.wait_ge(s["job_drained"], NJ * l + JOB["lT3"] + 1)
                scores(None, mla_q, mla_k, CAUSAL)
                p_transposes(6 * l + 3, CAUSAL)
                values(6 * l + 3, CAUSAL, mla_v, o64)
                pe.wait_ge(s["mix_ready"], l + 1)
                transposes(l, ["mix%d" % i for i in range(4)], lambda c, t: xn[:, t, c * P:c * P + P], DT)
                pe.wait_ge(s["job_drained"], NJ * l + JOB["mix3"] + 1)
                for u in range(2):
                    unit(l, U_OUT + u)
                    w = wide(U_OUT + u, 1024, 4)
                    for t in range(TT):
                        for hf in range(2):
                            for k in range(4):
                                last = pe.matmul(B(2 * t + hf), mT[:, 4 * u + k, t * P:t * P + P], w[:, k, 512 * hf:512 * hf + 512],
                                                 start=(u == 0 and k == 0), stop=(u == 1 and k == 3), skip_group_check=True)
                    last.then_inc(s["out_filled"], 1)
                for t in range(TT):
                    pe.wait_ge(s["xn_ready"], 4 * l + 2 + t + 1)
                transposes(l, ["post%d" % i for i in range(4)], lambda c, t: xn[:, t, c * P:c * P + P], DT)
                pe.wait_ge(s["job_drained"], NJ * l + JOB["post3"] + 1)
                for i, (kind, u) in enumerate(MLP_ORDER):
                    if kind == "up":
                        mlp_up(l, i, u)
                    else:
                        mlp_down(l, i, u)
                    if i < 12:
                        ada_sum(l, i)

            def job2(name):
                i = JOB2[name]
                if i >= 4:
                    pe.wait_ge(s2["job_drained"], i - 3)
                return B(i % 4)

            def filled2(ins):
                ins.then_inc(s2["job_filled"], 1)

            def drained2(name):
                pe.wait_ge(s2["job_drained"], JOB2[name] + 1)

            def transposes2(names, src):
                for i, nm in enumerate(names):
                    b = job2(nm)
                    for c in range(2 * i, 2 * i + 2):
                        for t in range(TT):
                            last = pe.transpose(b[:, (c % 2) * S + t * P:(c % 2) * S + t * P + P], src(c, t), ident[:, :])
                    filled2(last)

            def norm2(prefix, nth):
                pe.wait_ge(s2["xn_ready"], 2 * nth + 2)
                transposes2([prefix + str(i) for i in range(4)], lambda c, t: xn[:, t, c * P:c * P + P])

            def features(names, w, x=None):
                for i, nm in enumerate(names):
                    b = job2(nm)
                    for c in range(2 * i, 2 * i + 2):
                        for k in range(DT):
                            last = pe.matmul(b[:, (c % 2) * S:(c % 2) * S + S], w[:, k, c * P:c * P + P], hT[:, k, :], start=(k == 0), stop=(k == DT - 1))
                    filled2(last)

            def gate_row(names, n):
                pe.wait_ge(s2["diag_ready"], n)
                for i, nm in enumerate(names):
                    b = job2(nm)
                    for d in range(4):
                        last = pe.matmul(b[:, d * P:d * P + P], ones[:, :], dg_of[n - 1][:, 4 * i + d, :], start=True, stop=True)
                    filled2(last)

            dg_of = [dg_ab3, dg_m, dg_m, dg_m]

            def out_products(j0, slots, landed_of, x):
                for u in range(2):
                    j = j0 + u
                    pe.wait_ge(landed_of[j % slots], 16 * (j // slots + 1))
                    w = wide2(j, 1024, 4, slots)
                    for t in range(TT):
                        for hf in range(2):
                            for k in range(4):
                                last = pe.matmul(B(2 * t + hf), x[:, 4 * u + k, t * P:t * P + P], w[:, k, 512 * hf:512 * hf + 512],
                                                 start=(u == 0 and k == 0), stop=(u == 1 and k == 3), skip_group_check=True)
                    last.then_inc(s2["out_filled"], 1)

            pe.wait_ge(s2["rows_in"], 112)
            pe.wait_ge(s["x_done"], 5)
            pe.transpose(B(4)[:, 0:ROWS_A], rowsA[0:ROWS_A, :], ident[0:ROWS_A, 0:ROWS_A])
            pe.transpose(B(4)[:, P:P + 124], rowsB[0:124, :], ident[0:124, 0:124]).then_inc(s2["rows_ps"], 1)
            norm2("an", 0)
            drained2("an3")
            for j in range(AB_UNITS):
                pe.wait_ge(landed2[j], 16)
                features(["ab%d" % (2 * j + i) for i in range(2)], wide2(j, 512))
            for nm, ready, src in (("ln_mu", "u_ready", abx[2]), ("ln_var", "uc_ready", abx[4])):
                pe.wait_ge(s2[ready], 1)
                b = job2(nm)
                for c in range(4):
                    last = pe.matmul(b[:, 0:S], ones[:, :], src[:, c, :], start=(c == 0), stop=(c == 3))
                filled2(last)
                if nm == "ln_mu":
                    gate_dep = None
            gate_row(["gate0a", "gate0b"], 1)
            drained2("gate0b")
            pe.wait_ge(s2["ya_ready"], 1)
            pe.wait_ge(s2["yb_ready"], 1)
            out_products(AB_OUT, 6, landed2, mixT)

            def moe(i, prefix, nth, before):
                m = sM
                norm2(prefix, nth)
                gate_row_b45(i)
                drained2(prefix + "3")
                pe.wait_ge(s2["moe_small_in"], 64 * i + 64)
                for t in range(TT):
                    for k in range(DT):
                        last = pe.matmul(B(4)[:, 64 * t:64 * t + 36], hT[:, k, t * P:t * P + P], wr[:, k, :], start=(k == 0), stop=(k == DT - 1))
                last.then_inc(m["logits_ps"], 1)
                pe.wait_ge(m["sel_ready"], i + 1)
                pe.matmul(B(5)[:, 0:NE], earlier[:, :], sel_e[:, 0, :], start=True, stop=True)
                pe.matmul(B(5)[:, NE:2 * NE], ones[:, :], sel_e[:, 0, :], start=True, stop=False)
                pe.matmul(B(5)[:, NE:2 * NE], earlier[:, :], sel_e[:, 1, :], start=False, stop=True)
                pe.matmul(B(5)[:, 2 * NE:3 * NE], ones[:, :], sel_e[:, 0, :], start=True, stop=False)
                pe.matmul(B(5)[:, 2 * NE:3 * NE], ones[:, :], sel_e[:, 1, :], start=False, stop=True).then_inc(m["rank_ps"], 1)
                pe.wait_ge(m["zero_ready"], i + 1)
                for b in range(4):
                    pe.matmul(B(b), zeros, hT[:, 0:2, :].rearrange("p k s -> p (k s)"), start=True, stop=True, skip_group_check=True)
                pe.wait_ge(s2["gate_row_drained"], i + 1)
                if i == 0:
                    pe.sem_inc(m["g_filled"], 1)
                    pe.sem_inc(m["gathered"], 2)
                    pe.sem_inc(m["pg_filled"], 1)
                    pe.sem_inc(m["u_filled"], 1)
                    pe.sem_inc(m["y_filled"], 2)
                pe.wait_ge(m["passes_ready"], i + 1)
                n = pe.value_load(passes_i[i][0:1, 0:1], min_val=1, max_val=4)

                def scatter(t):
                    for hf in range(2):
                        last = pe.matmul(B(2 * t + hf), pgT[:, t * P:t * P + P], ye[:, 512 * hf:512 * hf + 512], start=False, stop=True,
                                         skip_group_check=True)
                    if t == 1:
                        last.then_inc(m["scattered"], 1)

                def product(b, x, w, kk, c0, name):
                    for k in range(kk):
                        for e in range(2):
                            h = slice(SLOTS * e, SLOTS * e + SLOTS)
                            last = pe.matmul(b[h, :], x[:, k, h], w[e][:, k, c0:c0 + 512], start=(k == 0), stop=(k == kk - 1))
                    last.then_inc(m[name], 1)

                X, T, G, U = B(4), B(5), B(6), B(7)
                wslot = [ring[:, j, :].rearrange("p (k n) -> p k n", k=4 if j % 3 == 2 else DT) for j in range(6)]
                with pe.Fori(0, n) as q:
                    with pe.Fori(0, PAIRS) as pr:
                        it = (q + before) * PAIRS + pr
                        pe.wait_ge(m["p_ready"], it + 1)
                        pe.wait_ge(m["pg_drained"], it + 1)
                        for hf, b in ((0, X), (1, T)):
                            for t in range(TT):
                                last = pe.matmul(b, pick[:, t, :], xn[:, t, 512 * hf:512 * hf + 512], start=(t == 0), stop=(t == TT - 1))
                            last.then_inc(m["gathered"], 1)
                        pe.wait_ge(m["y_drained"], 2 * it + 2)
                        scatter(0)
                        for hf, b in ((0, X), (1, T)):
                            pe.wait_ge(m["xg_drained"], 2 * it + hf + 1)
                            for d in range(4):
                                last = pe.transpose(b[:, d * P:d * P + P], xg[:, (4 * hf + d) * P:(4 * hf + d) * P + P], ident[:, :])
                            last.then_inc(m["xt_filled"], 1)
                        scatter(1)
                        pe.wait_ge(m["xt_drained_v"], it + 1)
                        pe.wait_ge(m["xt_drained_s"], it + 1)
                        for b, j, name in ((G, 0, "g_filled"), (U, 1, "u_filled")):
                            pe.wait_ge(landedM[j], 16 * it + 16)
                            pe.wait_ge(landedM[j + 3], 16 * it + 16)
                            product(b, xeT, (wslot[j], wslot[j + 3]), DT, 0, name)
                        for t in range(TT):
                            last = pe.transpose(X[:, t * P:t * P + P], pickg[:, t, :], ident[:, :])
                        last.then_inc(m["pg_filled"], 1)
                        pe.wait_ge(m["a_ready"], it + 1)
                        for k in range(4):
                            last = pe.transpose(T[:, k * P:k * P + P], aa[:, k * P:k * P + P], ident[:, :])
                        last.then_inc(m["at_filled"], 1)
                        pe.wait_ge(m["at_drained"], it + 1)
                        for j in (2, 5):
                            pe.wait_ge(landedM[j], 16 * it + 16)
                        product(G, aTe, (wslot[2], wslot[5]), 4, 0, "y_filled")
                        product(U, aTe, (wslot[2], wslot[5]), 4, 512, "y_filled")
                pe.wait_ge(m["y_drained"], 2 * PAIRS * (n + before) + 2)
                pe.wait_ge(m["pg_drained"], PAIRS * (n + before) + 1)
                scatter(0)
                scatter(1)
                return n

            def gate_row_b45(i):
                pe.wait_ge(s2["diag_ready"], 2 * i + 2)
                for b in range(2):
                    for d in range(4):
                        last = pe.matmul(B(6 + b)[:, d * P:d * P + P], ones[:, :], dg_m[:, 4 * b + d, :], start=True, stop=True)
                last.then_inc(s2["gate_row_filled"], 1)

            n0 = moe(0, "bn", 1, 0)

            norm2("cn", 2)
            gate_row(["gate1a", "gate1b"], 3)
            drained2("cn3")

            def cd_unit(j):
                pe.wait_ge(landed3[j % CD_RING], 16 * (j // CD_RING + 1))
                return wide2(j, COLS_OF_CD[j][1], DT, CD_RING)

            w = cd_unit(0)
            features(["qi"], w)
            b = job2("ki")
            for k in range(DT):
                pe.matmul(b[0:32, 0:S], w[:, k, 256:288], hT[:, k, :], start=(k == 0), stop=(k == DT - 1))
            for t in range(TT):
                for k in range(DT):
                    last = pe.matmul(b[:, S + 8 * t:S + 8 * t + 8], hT[:, k, t * P:t * P + P], w[:, k, 288:296], start=(k == 0), stop=(k == DT - 1))
            filled2(last)
            drained2("ki")
            for h in range(8):
                b = job2("rel%d" % h)
                for t in range(TT):
                    last = pe.matmul(b[:, S * t:S * t + S], qiT[0:32, h, t * P:t * P + P], kiT[0:32, :], start=True, stop=True)
                filled2(last)

            def natural2(names, w):
                for t, nm in enumerate(names):
                    b = job2(nm)
                    for k in range(DT):
                        last = pe.matmul(b, hT[:, k, t * P:t * P + P], w[:, k, :], start=(k == 0), stop=(k == DT - 1))
                    filled2(last)

            def scores2(g, q, kf):
                for i, heads in enumerate(FULL):
                    if g > 0:
                        pe.wait_ge(s2["pt_drained"], 4 * (g - 1) + i + 1)
                    for c, (h, t, _) in enumerate(heads):
                        last = pe.matmul(B(4 + i)[:, c * S:c * S + S], q(h)[:, t * P:t * P + P], kf(h), start=True, stop=True)
                    last.then_inc(s2["scores"], 1)

            def p_transposes2(g):
                for i in range(4):
                    pe.wait_ge(s2["exp_done"], 4 * g + i + 1)
                    for c in range(4):
                        last = pe.transpose(B(4 + i)[:, c * P:c * P + P], sc4[:, i, c * P:c * P + P], ident[:, :])
                    last.then_inc(s2["pt_filled"], 1)

            def values2(g, names, v, width):
                pe.wait_ge(s2["pt_drained"], 4 * g + 4)
                if width == 64:
                    b = job2(names[0])
                for t in range(TT):
                    if width == 128:
                        b = job2(names[t])
                    for hp in range(2):
                        i = 2 * t + hp
                        for c in range(2):
                            h = 2 * hp + c
                            o = b[:, 256 * t + 64 * h:256 * t + 64 * h + 64] if width == 64 else b[:, 128 * h:128 * h + 128]
                            for kt in range(TT):
                                last = pe.matmul(o, pT4[:, i, (2 * c + kt) * P:(2 * c + kt) * P + P], v(h, kt), start=(kt == 0), stop=(kt == TT - 1))
                    if width == 128:
                        filled2(last)
                if width == 64:
                    filled2(last)

            features(["qc0", "qc1"], cd_unit(1))
            features(["kc0", "kc1"], cd_unit(2))
            natural2(["vc0", "vc1"], cd_unit(3))
            features(["qd0", "qd1"], cd_unit(4))
            features(["kd0", "kd1"], cd_unit(5))
            natural2(["vd0", "vd1"], cd_unit(6))
            drained2("vd1")
            for g in range(4):
                if g < 2:
                    scores2(g, lambda h: qkC[0:64, 4 * g + h, :], lambda h: qkC[0:64, 8 + 4 * g + h, :])
                else:
                    scores2(g, lambda h: qkD[0:64, 2 * h + g - 2, :], lambda h: qkD[0:64, 8 + 2 * h + g - 2, :])
                p_transposes2(g)
                if g < 2:
                    values2(g, ["oc%d" % g], lambda h, kt: vcd[:, 0, kt, 64 * (4 * g + h):64 * (4 * g + h) + 64], 64)
                else:
                    values2(g, ["od%d%d" % (g - 2, t) for t in range(2)], lambda h, kt: vcd[:, 1, kt, 128 * h:128 * h + 128], 128)
            pe.wait_ge(s2["x_done"], 2)
            pe.wait_ge(s2["lam_ready"], 2)
            transposes2(["cm%d" % i for i in range(4)], lambda c, t: xn[:, t, c * P:c * P + P])
            drained2("cm3")
            out_products(CD_OUT, CD_RING, landed3, hT)
            moe(1, "dn", 3, n0)

        @block.scalar
        def _(act):
            own = Counter(act, s["act_own"])
            act.sem_inc(s["up_square"], 2)

            def drain(l, name, *copies):
                act.wait_ge(s["job_filled"], NJ * l + JOB[name] + 1)
                b = B(JOB[name] % 4)
                for i, (o, view, kw) in enumerate(copies):
                    kw = dict(kw)
                    ins = act.activation(o, view(b), kw.pop("func", ACT.Copy), **kw)
                ins.then_inc(s["job_drained"], 1)

            def drain_cols(l, names, dst, col, n=DT):
                for i, nm in enumerate(names):
                    act.wait_ge(s["job_filled"], NJ * l + JOB[nm] + 1)
                    b = B(JOB[nm] % 4)
                    for c in range(2 * i, min(2 * i + 2, n)):
                        ins = act.activation(dst[:, c, :], b[:, (c % 2) * S:(c % 2) * S + S], ACT.Copy, scale=colsC[:, col + c:col + c + 1])
                    ins.then_inc(s["job_drained"], 1)

            def pair(n=2):
                return lambda b: b[:, 0:n * S].rearrange("p (c s) -> p c s", c=n)

            def exps(g0, plan):
                for i, heads in enumerate(plan):
                    act.wait_ge(s["masked"], g0 + i + 1)
                    col = 0
                    for j, (h, t, kts) in enumerate(heads):
                        n = P * len(kts)
                        ins = act.activation(sc[:, i, col:col + n], sc[:, i, col:col + n], ACT.Exp, bias=nmx[:, i, j:j + 1],
                                             accum_out=esum[:, t, h:h + 1])
                        col += n
                    ins.then_inc(s["exp_done"], 1)

            def pt_drains(g0, plan):
                for i in range(len(plan)):
                    act.wait_ge(s["pt_filled"], g0 + i + 1)
                    act.activation(pT[:, i, :], B(ABANK[i]), ACT.Copy).then_inc(s["pt_drained"], 1)

            act.wait_ge(s["cols_ps"], 1)
            act.activation(cond[:, :], B(4)[:, 0:DT], ACT.Copy).then_inc(s["cols_sb"], 1)
            act.wait_ge(s["cols_sb"], 1)
            act.activation(stat[:, 0, 0:DT], cond[:, :], ACT.Tanh, scale=0.5).then_inc(s["cond_act"], 1)
            act.wait_ge(s["trig_dve"], 1)
            act.activation(trig[:, 6, :, :], trig[:, 4, :, :], ACT.Sin).then_inc(s["trig_act"], 1)
            act.activation(trig[:, 7, :, :], trig[:, 5, :, :], ACT.Sin).then_inc(s["trig_act"], 1)
            base = own.n

            with act.Fori(0, L1) as l:
                own.start(base + l * CHAIN)
                act.wait_ge(s["layer_rows_ps"], l + 1)
                act.activation(colsC[:, :], B(5)[:, 0:P], ACT.Copy).then_inc(s["layer_cols"], 1)
                act.wait_ge(s["layer_cols"], l + 1)
                drain_cols(l, ["norm%d" % i for i in range(4)], hT, R_MIX)
                for i in range(2):
                    drain(l, "qk%d" % i, (qkpad[:, 2 * i:2 * i + 2, 3:259], pair(), {}))
                drain(l, "gate", (rows[0], lambda b: b[0:HM, 0:S], {}), (rows[1], lambda b: b[32:32 + HM, 0:S], {}))
                for u, n in ((0, 512), (1, 512), (2, 416)):
                    for t in range(TT):
                        drain(l, "r%d%d" % (u, t), (qkv[:, t, 512 * u:512 * u + n], lambda b: b[:, 0:n], {}))
                    if u == 0:
                        act.wait_ge(s["conv_z"], l + 1)
                        act.activation(cv2[:, :, :], cv[:, :, :], ACT.Tanh, scale=0.5).then_inc(s["conv_tanh"], 1)
                    if u == 1:
                        act.wait_ge(s["gate_abs"], l + 1)
                        own.do(act.activation(rows[2], rows[2], ACT.Exp))
                        own.wait()
                        act.activation(rows[2], rows[2], ACT.Ln, bias=1.0).then_inc(s["gate_log"], 1)
                act.wait_ge(s["rows_ready"], l + 1)
                act.activation(rows[6], rows[6], ACT.Exp, scale=-1.0).then_inc(s["rows_exp"], 1)
                for i in range(2):
                    drain(l, "aT%d" % i, (aT[0:64, 4 * i:4 * i + 4:2, :], lambda b: b[0:64, :].rearrange("p (c s) -> p c s", c=2), {}),
                          (aT[0:64, 4 * i + 1:4 * i + 4:2, :], lambda b: b[64:128, :].rearrange("p (c s) -> p c s", c=2), {}))
                drain_cols(l, ["cT0", "cT1", "cT2"], cT, R_GCQ, 5)
                exps(6 * l, CAUSAL)
                drain(l, "gT", (gcol[:, :, :], lambda b: b[:, 0:4 * HM].rearrange("p (q h) -> p q h", h=HM), {}))
                for t in range(TT):
                    drain(l, "v%d" % t, (vext[:, t, :, 0:DV], lambda b: b[:, :].rearrange("p (h v) -> p h v", h=HM), {}))
                pt_drains(6 * l, CAUSAL)
                for t in range(TT):
                    drain(l, "lq%d" % t, (lqk[:, t, 0:HA, :], lambda b: b[:, 0:384].rearrange("p (h d) -> p h d", h=HA), {}))
                for t in range(TT):
                    drain(l, "lkv%d" % t,
                          (lqk[:, t, HA:8, 0:64], lambda b: b[:, :].rearrange("p (h d) -> p h d", h=HA)[:, :, 0:64], {}),
                          (lv[:, t, :, :], lambda b: b[:, :].rearrange("p (h d) -> p h d", h=HA)[:, :, 64:128], {}))
                for t in range(TT):
                    drain(l, "o%d" % t, (og[:, t, :], lambda b: b[:, :], {"func": ACT.Tanh, "scale": 0.5}))
                for i in range(4):
                    drain(l, "lT%d" % i, (lT[0:96, 2 * i:2 * i + 2, :], lambda b: b[0:96, :].rearrange("p (c s) -> p c s", c=2), {}))
                for h in range(HM):
                    act.wait_ge(s["m_arg"], 4 * l + h + 1)
                    e = sc[:, h % 2, :]
                    act.activation(e[:, 0:S], e[:, 0:S], ACT.Exp, bias=gcol[:, 0, h:h + 1])
                    act.activation(e[:, S:3 * P], e[:, S:3 * P], ACT.Exp, bias=gcol[:, 1, h:h + 1]).then_inc(s["m_exp"], 1)
                exps(6 * l + 3, CAUSAL)
                pt_drains(6 * l + 3, CAUSAL)
                drain_cols(l, ["mix%d" % i for i in range(4)], hT, R_GOUT)
                drain_cols(l, ["post%d" % i for i in range(4)], hT, R_MLP)
                for u in range(8):
                    for b in range(2):
                        act.wait_ge(s["up_filled"], 16 * l + 16 + 2 * u + b + 1)
                        own.do(act.activation(ru[:, b, :], B(4 + b), ACT.Relu))
                        own.wait()
                        act.activation(uT[:, u % 2, 2 * b:2 * b + 2, :], ru[:, b, :].rearrange("p (c s) -> p c s", c=2),
                                       ACT.Square).then_inc(s["up_square"], 1)
                own.pad()

            def j2(name):
                act.wait_ge(s2["job_filled"], JOB2[name] + 1)
                return B(JOB2[name] % 4)

            def out2(ins):
                ins.then_inc(s2["job_drained"], 1)

            def norm_drains(prefix, i):
                sh = modc[:, i // 2, 24 * (i % 2):24 * (i % 2) + 8]
                for q in range(4):
                    b = j2(prefix + str(q))
                    for c in range(2 * q, 2 * q + 2):
                        ins = act.activation(hT[:, c, :], b[:, (c % 2) * S:(c % 2) * S + S], ACT.Identity, scale=gm[:, i, c:c + 1], bias=sh[:, c:c + 1])
                    out2(ins)

            def two(b):
                return b.rearrange("p (c s) -> p c s", c=2)

            act.wait_ge(s2["rows_ps"], 1)
            act.activation(colsA[:, 0:ROWS_A], B(4)[:, 0:ROWS_A], ACT.Copy)
            act.activation(colsB[:, 0:124], B(4)[:, P:P + 124], ACT.Copy).then_inc(s2["cols_done"], 1)
            act.wait_ge(s2["cols_ready"], 1)
            norm_drains("an", 0)
            for u in range(AB_UNITS):
                for i in range(2):
                    b = j2("ab%d" % (2 * u + i))
                    out2(act.activation(abx[u][:, 2 * i:2 * i + 2, :], two(b), ACT.Tanh if u == 4 else ACT.Copy, scale=0.5 if u >= 3 else 1.0))
            b = j2("ln_mu")
            out2(act.activation(mu, b[:, 0:S], ACT.Copy, scale=1.0 / 512))
            b = j2("ln_var")
            act.wait_ge(s2["cols_ready"], 1)
            ins = act.activation(var, b[:, 0:S], ACT.Sqrt, scale=1.0 / 512, bias=lnsq)
            out2(ins)
            for i in range(2):
                b = j2("gate0" + "ab"[i])
                out2(act.activation(gbc2[:, 512 * i:512 * i + 512], b, ACT.Copy))
            act.wait_ge(s2["zb_ready"], 1)
            for c in range(4):
                ins = act.activation(abx[2][:, c, :], abx[2][:, c, :], ACT.Identity, scale=half_cols[:, c:c + 1], bias=half_cols[:, 4 + c:5 + c])
            own.start(base + L1 * CHAIN)
            own.do(ins)
            own.wait()
            act.activation(abx[4][:, :, :], abx[2][:, :, :], ACT.Tanh).then_inc(s2["zb_tanh"], 1)

            def moe(i, prefix, before):
                m = sM
                norm_drains(prefix, 2 * i + 1)
                act.wait_ge(s2["gate_row_filled"], i + 1)
                for b in range(2):
                    ins = act.activation(gbc2[:, 512 * b:512 * b + 512], B(6 + b), ACT.Copy)
                ins.then_inc(s2["gate_row_drained"], 1)
                act.wait_ge(m["exp_in"], 2 * i + 1)
                act.activation(fx[:, :, 0:4], fx[:, :, 0:4], ACT.Exp).then_inc(m["exp_out"], 1)
                act.wait_ge(m["exp_in"], 2 * i + 2)
                act.activation(rsm[:, 8:10], rsm[:, 8:10], ACT.Exp).then_inc(m["exp_out"], 1)
                if i == 0:
                    act.sem_inc(m["y_drained"], 2)
                    act.sem_inc(m["pg_drained"], 1)
                act.wait_ge(m["passes_ready"], i + 1)
                n = act.value_load(passes_i[i][0:1, 0:1], min_val=1, max_val=4)
                sh = modc[:, i, 24:32]
                X, T, G, U = B(4), B(5), B(6), B(7)
                with act.Fori(0, n) as q:
                    with act.Fori(0, PAIRS) as pr:
                        it = (q + before) * PAIRS + pr
                        for hf, b in ((0, X), (1, T)):
                            act.wait_ge(m["gathered"], 2 * it + hf + 3)
                            act.activation(xg[:, 512 * hf:512 * hf + 512], b, ACT.Copy).then_inc(m["xg_drained"], 1)
                        act.wait_ge(m["xt_filled"], 2 * it + 2)
                        for d in range(4, 8):
                            ins = act.activation(xeT[:, d, :], T[:, (d - 4) * P:(d - 3) * P], ACT.Identity, scale=gm[:, 2 * i + 1, d:d + 1],
                                                 bias=sh[:, d:d + 1])
                        ins.then_inc(m["xt_drained_s"], 1)
                        act.wait_ge(m["g_filled"], it + 2)
                        act.wait_ge(m["g_free"], it + 1)
                        act.activation(th, G, ACT.Tanh, scale=0.5).then_inc(m["tanh_done"], 1)
                        act.wait_ge(m["pg_filled"], it + 2)
                        act.activation(pgT, X[:, 0:2 * P], ACT.Copy).then_inc(m["pg_drained"], 1)
                        for hf, b in ((0, G), (1, U)):
                            act.wait_ge(m["y_filled"], 2 * it + hf + 3)
                            act.activation(ye[:, 512 * hf:512 * hf + 512], b, ACT.Copy).then_inc(m["y_drained"], 1)
                return n

            n0 = moe(0, "bn", 0)
            norm_drains("cn", 2)
            for i in range(2):
                b = j2("gate1" + "ab"[i])
                out2(act.activation(gbc2[:, 512 * i:512 * i + 512], b, ACT.Copy))
            b = j2("qi")
            for r in range(4):
                ins = act.activation(qiT[0:32, r:r + 5:4, :], two(b)[32 * r:32 * r + 32], ACT.Copy)
            out2(ins)
            b = j2("ki")
            act.activation(kiT[0:32, :], b[0:32, 0:S], ACT.Copy)
            out2(act.activation(wix[:, :, :], b[:, S:S + 16].rearrange("p (t h) -> p t h", t=TT), ACT.Copy))
            for h in range(8):
                b = j2("rel%d" % h)
                if h >= 4:
                    act.wait_ge(s2["rel_used"], h - 3)
                out2(act.activation(sc4[:, h % 4, :], b, ACT.Relu))

            def halves(name, dst, first):
                b = j2(name)
                act.activation(dst[0:64, first:first + 3:2, :], two(b)[0:64], ACT.Copy)
                out2(act.activation(dst[0:64, first + 1:first + 4:2, :], two(b)[64:128], ACT.Copy))

            for i, dst in enumerate((qkC, qkD)):
                for k, nm in enumerate(("q", "k")):
                    for half in range(2):
                        halves("%s%s%d" % (nm, "cd"[i], half), dst, 8 * k + 4 * half)
                for t in range(TT):
                    b = j2("v%s%d" % ("cd"[i], t))
                    out2(act.activation(vcd[:, i, t, :], b, ACT.Copy))
            act.wait_ge(s2["lam_ready"], 1)
            act.activation(lam[:, 0:2], lam[:, 0:2], ACT.Exp).then_inc(s2["lam_exp"], 1)
            for g in range(4):
                for i, heads in enumerate(FULL):
                    act.wait_ge(s2["masked"], 4 * g + i + 1)
                    for c, (h, t, _) in enumerate(heads):
                        ins = act.activation(sc4[:, i, c * S:c * S + S], sc4[:, i, c * S:c * S + S], ACT.Exp, bias=nmx[:, i, c:c + 1],
                                             accum_out=esum[:, t, h:h + 1])
                    ins.then_inc(s2["exp_done"], 1)
                for i in range(4):
                    act.wait_ge(s2["pt_filled"], 4 * g + i + 1)
                    act.activation(pT4[:, i, :], B(4 + i), ACT.Copy).then_inc(s2["pt_drained"], 1)
                if g < 2:
                    b = j2("oc%d" % g)
                    out2(act.activation(xn[:, :, 256 * g:256 * g + 256], b.rearrange("p (t n) -> p t n", t=TT), ACT.Copy))
                else:
                    for t in range(TT):
                        b = j2("od%d%d" % (g - 2, t))
                        out2(act.activation(xn[:, t, 512:1024] if g == 2 else od2[:, t, :], b, ACT.Copy))
            for q in range(4):
                b = j2("cm%d" % q)
                for c in range(2 * q, 2 * q + 2):
                    ins = act.activation(hT[:, c, :], b[:, (c % 2) * S:(c % 2) * S + S], ACT.Copy, scale=dcol if c >= 4 else 1.0)
                out2(ins)
            moe(1, "dn", n0)

        @block.vector
        def _(dve):
            own = Counter(dve, s["dve_own"])
            do, wait = own.do, own.wait

            def norm_rows(l, name, view, width, tiles):
                i = STAT[name]
                n = len(tiles)
                for k, (src, w) in enumerate(view):
                    pass

            def squares(l, name, src, groups, width):
                sq = tmp[:, 0:TT * groups * width].rearrange("p (t g w) -> p t g w", t=TT, g=groups)
                wait()
                do(dve.tensor_tensor(sq, src, src, ALU.mult))
                wait()
                nn = TT * groups * width // 8
                do(dve.tensor_reduce(sq8[:, 0:nn], tmp[:, 0:TT * groups * width].rearrange("p (n w) -> p n w", w=8), AX_X, ALU.add))
                wait()
                dve.tensor_reduce(stat[:, STAT[name], 0:TT * groups], sq8[:, 0:nn].rearrange("p (n w) -> p n w", w=width // 8), AX_X, ALU.add).then_inc(s["stat_ready"], 1)
                dve.wait_ge(s["stat_ready"], len(STATS) * l + STAT[name] + 1)

            def full_squares(l, name):
                wait()
                do(dve.tensor_tensor(xn[:, :, :], xres[:, :, :], xres[:, :, :], ALU.mult))
                wait()
                do(dve.tensor_reduce(tmp[:, 0:64].rearrange("p (t g) -> p t g", t=TT), xn[:, :, :].rearrange("p t (g w) -> p t g w", g=32), AX_X, ALU.add))
                wait()
                ins = dve.tensor_reduce(stat[:, STAT[name], 0:TT], tmp[:, 0:64].rearrange("p (t g) -> p t g", t=TT), AX_X, ALU.add)
                ins.then_inc(s["stat_ready"], 1)
                dve.wait_ge(s["stat_ready"], len(STATS) * l + STAT[name] + 1)

            def rs(l, name):
                dve.wait_ge(s["rstd_ready"], len(STATS) * l + STAT[name] + 1)
                return rstd[:, STAT[name], :]

            def norm_x(l, name, nth):
                full_squares(l, name)
                r = rs(l, name)
                for t in range(TT):
                    dve.tensor_scalar(xn[:, t, :], xres[:, t, :], r[:, t:t + 1], None, ALU.mult).then_inc(s["xn_ready"], 1)

            def per_group(dst, src, r, groups, width):
                r4 = r[:, 0:TT * groups].rearrange("p (t g) -> p t g", t=TT)
                return dve.tensor_tensor(dst, src, spread(r4, 3, width), ALU.mult)

            def rope(x, half, c0):
                heads = x.shape[2]
                t4 = [tmp[:, i * 256:i * 256 + TT * heads * half].rearrange("p (t h d) -> p t h d", t=TT, h=heads) for i in range(4)]
                sn = spread(trig[:, 6, :, c0:c0 + half], 2, heads)
                cs = spread(trig[:, 7, :, c0:c0 + half], 2, heads)
                x1, x2 = x[:, :, :, 0:half], x[:, :, :, half:2 * half]
                wait()
                do(dve.tensor_tensor(t4[0], x1, cs, ALU.mult))
                do(dve.tensor_tensor(t4[1], x2, sn, ALU.mult))
                do(dve.tensor_tensor(t4[2], x2, cs, ALU.mult))
                do(dve.tensor_tensor(t4[3], x1, sn, ALU.mult))
                wait()
                do(dve.tensor_tensor(x1, t4[0], t4[1], ALU.subtract))
                return dve.tensor_tensor(x2, t4[2], t4[3], ALU.add)

            def logits(g0, plan, scale, mask):
                for i, heads in enumerate(plan):
                    dve.wait_ge(s["scores"], g0 + i + 1)
                    n = P * len(heads[0][2])
                    k = len(heads)
                    view = B(ABANK[i])[:, 0:k * n].rearrange("p (h n) -> p h n", h=k)
                    dst = sc[:, i, 0:k * n].rearrange("p (h n) -> p h n", h=k)
                    do(dve.scalar_tensor_tensor(dst, view, scale, mask(i, heads, n), ALU.mult, ALU.add))
                    wait()
                    do(dve.tensor_reduce(nmx[:, i, 0:k], dst, AX_X, ALU.max, negate=True))
                    wait()
                    dve.tensor_scalar(nmx[:, i, 0:k], nmx[:, i, 0:k], SHIFT, None, ALU.add).then_inc(s["masked"], 1)

            def causal(i, heads, n):
                m = qmask[:, P:S] if i == 0 else qmask[:, :]
                return spread(m, 1, len(heads))

            def attention_out(g, g0, plan, dst, width, o_of):
                dve.wait_ge(s["exp_done"], g0 + len(plan))
                do(dve.reciprocal(rsum[:, :, :], esum[:, :, :]))
                wait()
                dve.wait_ge(s["pv_done"], g + 1)
                r = spread(rsum[:, :, :], 3, width)
                for t in range(TT):
                    ins = dve.tensor_tensor(dst[:, t], o_of(t), r[:, t], ALU.mult)
                    if t == 0:
                        do(ins)
                ins.then_inc(s["o_done"], 1)
                dve.wait_ge(s["o_done"], g + 1)

            def o64(t):
                return B(7)[:, 256 * t:256 * t + 256].rearrange("p (h d) -> p h d", h=HA)

            def heads_of(x, c, n, w):
                return x[:, :, c:c + n * w].rearrange("p t (h d) -> p t h d", h=n)

            dve.wait_ge(s["consts"], 1)
            dve.wait_ge(s["tokens_pos"], 16)
            do(dve.tensor_copy(posn[:, :], posi[:, :]))
            wait()
            T = [trig[:, i, :, :] for i in range(8)]
            do(dve.tensor_tensor(T[1], T[0], spread(posn[:, :], 2, 24), ALU.mult))
            wait()
            do(dve.tensor_scalar(T[2], T[1], 1.0 / (2 * np.pi), None, ALU.mult))
            wait()
            do(dve.tensor_scalar(T[3], T[2], ROUND, None, ALU.add))
            wait()
            do(dve.tensor_scalar(T[2], T[3], ROUND, None, ALU.subtract))
            wait()
            for c, (src, dst) in zip((TWO_PI_A, TWO_PI_B, TWO_PI_C), ((1, 3), (3, 4), (4, 3))):
                do(dve.scalar_tensor_tensor(T[dst], T[2], -c, T[src], ALU.mult, ALU.add))
                wait()
            do(dve.tensor_scalar(T[4], T[3], 3.1415925, -3.1415925, ALU.min, ALU.max))
            wait()
            do(dve.scalar_tensor_tensor(T[2], T[4], -1.0, T[4], ALU.mult, ALU.max))
            wait()
            dve.tensor_scalar(T[5], T[2], -1.0, float(np.pi / 2), ALU.mult, ALU.add).then_inc(s["trig_dve"], 1)
            dve.wait_ge(s["cond_act"], 1)
            do(dve.scalar_tensor_tensor(cond[:, :], stat[:, 0, 0:DT], 1.0, cond[:, :], ALU.add, ALU.mult))
            wait()
            do(dve.tensor_scalar(cond[:, :], cond[:, :], 0.5, None, ALU.mult))
            wait()
            dve.wait_ge(s["trig_act"], 2)
            dve.wait_ge(s["x_in"], 16)
            base = own.n

            with dve.Fori(0, L1) as l:
                own.start(base + l * CHAIN)
                norm_x(l, "norm", 0)
                dve.wait_ge(s["layer_cols"], l + 1)
                dve.wait_ge(s["job_drained"], NJ * l + JOB["qk1"] + 1)
                for w in range(4):
                    for c in range(4):
                        col = colsC[:, R_CW + 4 * w + c:R_CW + 4 * w + c + 1]
                        if w == 0:
                            ins = dve.tensor_scalar(cv[:, c, :], qkpad[:, c, 0:S], col, colsC[:, R_CB + c:R_CB + c + 1], ALU.mult, ALU.add)
                        else:
                            ins = dve.scalar_tensor_tensor(cv[:, c, :], qkpad[:, c, w:w + S], col, cv[:, c, :], ALU.mult, ALU.add)
                        if w < 3 or c < 3:
                            do(ins)
                    if w < 3:
                        wait()
                wait()
                ins.then_inc(s["conv_z"], 1)
                R = rows
                dve.wait_ge(s["layer_small_in"], 128 * l + 128)
                dve.wait_ge(s["job_drained"], NJ * l + JOB["gate"] + 1)
                do(dve.tensor_scalar(R[0], R[0], bif[:, 0:1], None, ALU.add))
                do(dve.tensor_scalar(R[1], R[1], bif[:, 1:2], None, ALU.add))
                wait()
                dve.scalar_tensor_tensor(R[2], R[1], -1.0, R[1], ALU.mult, ALU.min).then_inc(s["gate_abs"], 1)
                dve.wait_ge(s["conv_tanh"], l + 1)
                dve.scalar_tensor_tensor(qkT[:, :, :].rearrange("p c s -> p (c s)"), cv2[:, :, :].rearrange("p c s -> p (c s)"), 1.0,
                                         cv[:, :, :].rearrange("p c s -> p (c s)"), ALU.add, ALU.mult).then_inc(s["qk_act"], 1)
                dve.wait_ge(s["job_drained"], NJ * l + JOB["r01"] + 1)
                qk = heads_of(qkv, 0, 8, 64)
                squares(l, "moba", qk, 8, 64)
                dve.wait_ge(s["gate_log"], l + 1)
                do(dve.scalar_tensor_tensor(R[1], R[1], 0.0, R[2], ALU.min, ALU.subtract))
                wait()
                do(dve.tensor_tensor_scan(R[3], R[1], R[7], 0.0, ALU.add, ALU.add))
                wait()
                do(dve.tensor_tensor(R[5], R[0], R[3], ALU.subtract))
                wait()
                do(dve.tensor_tensor_scan(R[6], R[5], R[5], 0.0, ALU.max, ALU.max))
                wait()
                do(dve.tensor_scalar(R[4], R[6], -1.0, None, ALU.mult))
                wait()
                dve.scalar_tensor_tensor(R[6], R[6], -M_SHIFT, R[3], ALU.add, ALU.add).then_inc(s["rows_ready"], 1)
                dve.wait_ge(s["job_drained"], NJ * l + JOB["r21"] + 1)
                for i, (c, w) in enumerate(((CQ, 384), (CKV, 256))):
                    for t in range(TT):
                        ins = dve.tensor_tensor_reduce(tmp[:, 0:w], qkv[:, t, c:c + w], qkv[:, t, c:c + w], 1.0, 0.0, ALU.mult, ALU.add,
                                                       stat[:, STAT["lora"], 2 * i + t:2 * i + t + 1])
                        if (i, t) != (1, 1):
                            do(ins)
                            wait()
                ins.then_inc(s["stat_ready"], 1)
                dve.wait_ge(s["stat_ready"], len(STATS) * l + STAT["lora"] + 1)
                r = rs(l, "moba")
                do(per_group(qk, qk, r, 8, 64))
                wait()
                for half in range(2):
                    part = heads_of(qkv, 256 * half, 4, 64)
                    for t in range(TT):
                        do(dve.tensor_tensor(part[:, t], part[:, t], spread(gbc[:, 64 * half:64 * half + 64], 1, 4), ALU.mult))
                rope(qk[:, :, :, 0:16], 8, 0).then_inc(s["aqk_ready"], 1)
                r = rs(l, "lora")
                for i, (c, w) in enumerate(((CQ, 384), (CKV, 256))):
                    for t in range(TT):
                        ins = dve.tensor_scalar(qkv[:, t, c:c + w], qkv[:, t, c:c + w], r[:, 2 * i + t:2 * i + t + 1], None, ALU.mult)
                        if (i, t) != (1, 1):
                            do(ins)
                wait()
                ins.then_inc(s["lora_ready"], 1)
                logits(6 * l, CAUSAL, 64 ** -0.5, causal)
                dve.wait_ge(s["job_drained"], NJ * l + JOB["lkv1"] + 1)
                for t in range(TT):
                    do(dve.tensor_copy(lqk[:, t, HA:8, 64:96], spread(qkv[:, t, KPE:KPE + 32], 1, HA)))
                squares(l, "mla", lqk[:, :, :, :], 8, 96)
                mo = heads_of(xn, 512, 4, 64)
                attention_out(2 * l, 6 * l, CAUSAL, mo, 64, o64)
                r = rs(l, "mla")
                do(per_group(lqk[:, :, :, :], lqk[:, :, :, :], r, 8, 96))
                wait()
                for half in range(2):
                    for t in range(TT):
                        do(dve.tensor_tensor(lqk[:, t, 4 * half:4 * half + 4, :], lqk[:, t, 4 * half:4 * half + 4, :],
                                             spread(gbc[:, 128 + 96 * half:224 + 96 * half], 1, 4), ALU.mult))
                rope(lqk[:, :, :, 64:96], 16, 8).then_inc(s["lqk_ready"], 1)
                squares(l, "moba_out", mo, 4, 64)
                for h0 in (0, 2):
                    for h in (h0, h0 + 1):
                        dve.wait_ge(s["m_bc"], 2 * l + h // 2 + 1)
                        bc = B(6 + h // 2)[:, (h % 2) * S:(h % 2) * S + S]
                        e = sc[:, h % 2, :]
                        do(dve.tensor_tensor(e[:, 0:S], bc, smask[:, 0:S], ALU.add))
                        ins = dve.tensor_tensor(e[:, S:3 * P], bc[:, P:S], smask[:, S:3 * P], ALU.add)
                        wait()
                        ins.then_inc(s["m_arg"], 1)
                    for h in (h0, h0 + 1):
                        dve.wait_ge(s["m_s"], 4 * l + h + 1)
                        dve.wait_ge(s["m_exp"], 4 * l + h + 1)
                        dve.scalar_tensor_tensor(pT[:, h % 2, 0:3 * P], B(4 + h % 2)[:, 0:3 * P], DQK ** -0.5 / 4, sc[:, h % 2, 0:3 * P],
                                                 ALU.mult, ALU.mult).then_inc(s["m_p"], 1)
                    for h in (h0, h0 + 1):
                        dve.wait_ge(s["m_num"], 4 * l + h + 1)
                        num = B(4 + h % 2)[:, 0:258].rearrange("p (t v) -> p t v", t=TT)
                        den = tmp[:, 1024:1026]
                        do(dve.tensor_copy(den.unsqueeze(2), num[:, :, 128:129]))
                        wait()
                        do(dve.scalar_tensor_tensor(tmp[:, 1028:1030], den, -1.0, den, ALU.mult, ALU.max))
                        wait()
                        do(dve.tensor_tensor(tmp[:, 1032:1034], tmp[:, 1028:1030], gcol[:, 2:4, h], ALU.max))
                        wait()
                        do(dve.reciprocal(tmp[:, 1036:1038], tmp[:, 1032:1034]))
                        wait()
                        dve.tensor_tensor(xn[:, :, DV * h:DV * h + DV], num[:, :, 0:DV], spread(tmp[:, 1036:1038], 2, DV),
                                          ALU.mult).then_inc(s["m_h"], 1)
                dve.wait_ge(s["m_h"], 4 * l + 4)
                hm = heads_of(xn, 0, HM, DV)
                squares(l, "mlstm_out", hm, HM, DV)
                do(dve.tensor_scalar(og[:, :, :], og[:, :, :], 1.0, 0.5, ALU.add, ALU.mult))
                do(per_group(mo, mo, rs(l, "moba_out"), 4, 64))
                logits(6 * l + 3, CAUSAL, 96 ** -0.5, causal)
                do(per_group(hm, hm, rs(l, "mlstm_out"), HM, DV))
                wait()
                do(dve.tensor_tensor(xn[:, :, 0:512], xn[:, :, 0:512], og[:, :, :], ALU.mult))
                ml = heads_of(xn, 768, 4, 64)
                attention_out(2 * l + 1, 6 * l + 3, CAUSAL, ml, 64, o64)
                squares(l, "mla_out", ml, 4, 64)
                wait()
                per_group(ml, ml, rs(l, "mla_out"), 4, 64).then_inc(s["mix_ready"], 1)
                dve.wait_ge(s["out_filled"], 2 * l + 2)
                for t in range(TT):
                    ins = dve.tensor_tensor(xres[:, t, :], xres[:, t, :], bank[:, 2 * t:2 * t + 2, :].rearrange("p b n -> p (b n)"), ALU.add)
                    if t == 0:
                        do(ins)
                wait()
                ins.then_inc(s["x_done"], 1)
                dve.wait_ge(s["x_done"], 2 * l + 3)
                norm_x(l, "post", 1)
                for c in range(13):
                    if c < 12:
                        for hf in range(2):
                            dve.wait_ge(ada_in[hf], 16 * 12 * l + 16 * (c + 1))
                            for k in range(4):
                                kk = 4 * hf + k
                                if kk == 0:
                                    ins = dve.tensor_scalar(ada_acc[:, c % 2, :], ada_w[hf][:, k, :], cond[:, kk:kk + 1], None, ALU.mult)
                                else:
                                    ins = dve.scalar_tensor_tensor(ada_acc[:, c % 2, :], ada_w[hf][:, k, :], cond[:, kk:kk + 1],
                                                                   ada_acc[:, c % 2, :], ALU.mult, ALU.add)
                                if k < 3:
                                    do(ins)
                                    wait()
                            ins.then_inc(s["ada_acc"], 1)
                            dve.wait_ge(s["ada_acc"], 24 * l + 2 * c + hf + 3)
                    if c > 0:
                        c1 = c - 1
                        dve.wait_ge(s["ada_filled"], 12 * l + c)
                        dve.tensor_copy(modc[:, l, 4 * c1:4 * c1 + 4], B(6)[:, 0:4]).then_inc(s["ada_drained"], 1)
                dve.wait_ge(s["down_done"], 8 * l + 16)
                for t in range(TT):
                    ins = dve.tensor_tensor(xres[:, t, :], xres[:, t, :], bank[:, 2 * t:2 * t + 2, :].rearrange("p b n -> p (b n)"), ALU.add)
                    if t == 0:
                        do(ins)
                wait()
                ins.then_inc(s["x_done"], 1)
                dve.wait_ge(s["x_done"], 2 * l + 4)
                own.pad()

            own.start(base + L1 * CHAIN)
            n_stat = [0]

            def stat_out(ins):
                n = n_stat[0]
                n_stat[0] += 1
                ins.then_inc(s2["stat_ready"], 1)
                dve.wait_ge(s2["rstd_ready"], n + 1)
                return rstd[:, n % len(STATS), :]

            def stat_col():
                return stat[:, n_stat[0] % len(STATS), :]

            def norm_x2(signal=True):
                wait()
                do(dve.tensor_tensor_reduce(xn[:, 0, :], xres[:, 0, :], xres[:, 0, :], 1.0, 0.0, ALU.mult, ALU.add, stat_col()[:, 0:1]))
                wait()
                r = stat_out(dve.tensor_tensor_reduce(xn[:, 1, :], xres[:, 1, :], xres[:, 1, :], 1.0, 0.0, ALU.mult, ALU.add, stat_col()[:, 1:2]))
                for t in range(TT):
                    ins = dve.tensor_scalar(xn[:, t, :], xres[:, t, :], r[:, t:t + 1], None, ALU.mult)
                    ins.then_inc(s2["xn_ready"], 1)

            def diag(dst, layer, c0):
                for d in range(DT):
                    ins = dve.tensor_scalar(dst[:, d, :], ident[:, :], modc[:, layer, c0 + d:c0 + d + 1], None, ALU.mult)
                    if d < DT - 1:
                        do(ins)
                wait()
                ins.then_inc(s2["diag_ready"], 1)

            def residual(n, scratch):
                for t in range(TT):
                    do(dve.tensor_tensor(scratch[t], bank[:, 2 * t:2 * t + 2, :].rearrange("p b n -> p (b n)"), gbc2, ALU.mult))
                wait()
                for t in range(TT):
                    ins = dve.tensor_tensor(xres[:, t, :], xres[:, t, :], scratch[t], ALU.add)
                    if t == 0:
                        do(ins)
                wait()
                ins.then_inc(s2["x_done"], 1)
                dve.wait_ge(s2["x_done"], n)

            norm_x2()
            dve.wait_ge(s2["cols_done"], 1)
            for i in range(4):
                do(dve.scalar_tensor_tensor(gm[:, i, :], modc[:, i // 2, 24 * (i % 2) + 8:24 * (i % 2) + 16], 1.0, colsA[:, A_NORM + 8 * i:A_NORM + 8 * i + 8],
                                            ALU.add, ALU.mult))
            do(dve.tensor_scalar(half_cols, colsA[:, A_LNG:A_LNG + 8], 0.5, None, ALU.mult))
            do(dve.memset(lnsq, EPS))
            dve.wait_ge(s2["small_in"], 64)
            do(dve.tensor_scalar(dcol, colsA[:, A_DG:A_DG + 1], 1.0 - LAMBDA_INIT, None, ALU.mult))
            wait()
            dve.sem_inc(s2["cols_ready"], 1)
            dist, dtmp = bkt.rearrange("p (t n) -> p t n", t=TT), cmask
            do(dve.tensor_copy(posr, with_i.bitcast(I32)))
            do(dve.tensor_copy(posq, posi[:, :]))
            wait()
            for t in range(TT):
                do(dve.tensor_scalar(dist[:, t, :], posr, -1.0, posq[:, t:t + 1], ALU.mult, ALU.add))
            wait()
            fl = lambda x: x.rearrange("p t n -> p (t n)")
            acc = abx[0][:, :, :].rearrange("p c s -> p (c s)")[:, 0:512]
            do(dve.tensor_scalar(fl(cmask), bkt, 0.0, NEG, ALU.is_lt, ALU.mult))
            do(dve.tensor_scalar(mu_var, bkt, 0.0, 16.0, ALU.max, ALU.min))
            wait()
            for k, thr in enumerate(THRESHOLDS):
                do(dve.scalar_tensor_tensor(mu_var, bkt, float(thr), mu_var, ALU.is_ge, ALU.add))
                wait()
            do(dve.tensor_copy(bkt, mu_var))
            for h in range(12):
                do(dve.tensor_copy(bias[:, h, :, :], cmask[:, :, :]))
            lr = lam_r.rearrange("p (i j d) -> p i j d", i=2, j=2)
            do(dve.tensor_tensor(lam_r[:, 0:64], lam_r[:, 0:64], lam_r[:, 64:128], ALU.mult))
            do(dve.tensor_tensor(lam_r[:, 128:192], lam_r[:, 128:192], lam_r[:, 192:256], ALU.mult))
            wait()
            dve.tensor_reduce(lam[:, 0:2], lr[:, :, 0, :], AX_X, ALU.add).then_inc(s2["lam_ready"], 1)

            def drained(name):
                dve.wait_ge(s2["job_drained"], JOB2[name] + 1)

            def conv(dst, src, taps, col, bias_col, ready):
                for w in range(taps):
                    for c in range(4):
                        cc = col(w, c)
                        if w == 0 and bias_col is None:
                            ins = dve.tensor_scalar(dst[:, c, :], src[:, c, 0:S], cc, None, ALU.mult)
                        elif w == 0:
                            ins = dve.tensor_scalar(dst[:, c, :], src[:, c, 0:S], cc, bias_col(c), ALU.mult, ALU.add)
                        else:
                            ins = dve.scalar_tensor_tensor(dst[:, c, :], src[:, c, w:w + S], cc, dst[:, c, :], ALU.mult, ALU.add)
                        if (w, c) != (taps - 1, 3):
                            do(ins)
                    if w < taps - 1:
                        wait()
                return ins

            dve.wait_ge(s2["pos_ready"], 1)
            drained("ab5")
            do(dve.tensor_tensor(pa[:, :, 2:2 + S], abx[1][:, :, :], abx[2][:, :, :], ALU.mult))
            wait()
            do(conv(abx[1], pa, 3, lambda w, c: colsA[:, A_CA + 4 * w + c:A_CA + 4 * w + c + 1], None, None))
            wait()
            do(dve.tensor_tensor(mixT[:, 0:4, :], abx[1][:, :, :], abx[0][:, :, :], ALU.mult))
            drained("ab9")
            do(dve.scalar_tensor_tensor(pb[:, :, 30:30 + S], abx[4][:, :, :], 1.0, abx[3][:, :, :], ALU.add, ALU.mult))
            wait()
            dve.sem_inc(s2["ya_ready"], 1)
            ins = conv(abx[2], pb, 31, lambda w, c: colsB[:, 4 * w + c:4 * w + c + 1], lambda c: colsA[:, A_BIAS + c:A_BIAS + c + 1], None)
            wait()
            ins.then_inc(s2["u_ready"], 1)
            drained("ln_mu")
            do(dve.tensor_tensor(abx[2][:, :, :], abx[2][:, :, :], spread(mu, 1, 4), ALU.subtract))
            wait()
            dve.tensor_tensor(abx[4][:, :, :], abx[2][:, :, :], abx[2][:, :, :], ALU.mult).then_inc(s2["uc_ready"], 1)
            drained("ln_var")
            diag(dg_ab3, 0, 16)
            do(dve.reciprocal(var, var))
            wait()
            dve.tensor_tensor(abx[2][:, :, :], abx[2][:, :, :], spread(var, 1, 4), ALU.mult).then_inc(s2["zb_ready"], 1)
            dve.wait_ge(s2["zb_tanh"], 1)
            dve.scalar_tensor_tensor(mixT[:, 4:8, :], abx[4][:, :, :], 1.0, abx[2][:, :, :], ALU.add, ALU.mult).then_inc(s2["yb_ready"], 1)
            dve.wait_ge(s2["out_filled"], 2)
            drained("gate0b")
            residual(1, [region(0, 1024), region(1024, 1024)])

            def first_hot(dst, vals, top, n, m):
                do(dve.tensor_tensor(fk[:, :, 0:n], vals, spread(top, 2, n), ALU.is_equal))
                wait()
                do(dve.tensor_tensor(fk[:, :, 0:n], fk[:, :, 0:n], desc[:, :, 0:n], ALU.mult))
                wait()
                do(dve.tensor_reduce(rsm[:, 20:22], fk[:, :, 0:n], AX_X, ALU.max))
                wait()
                do(dve.tensor_tensor(dst, desc[:, :, 0:n], spread(rsm[:, 20:22], 2, n), ALU.is_equal))
                wait()

            def moe(i, with_bias, before):
                m = sM
                mo = Counter(dve, m["own_loop"])
                norm_x2()
                diag(dg_m, i, 40)
                do(dve.memset(zeros, 0.0))
                do(dve.memset(ye, 0.0))
                do(dve.memset(pgT, 0.0))
                wait()
                dve.sem_inc(m["zero_ready"], 1)
                for t in range(TT):
                    do(dve.tensor_scalar(desc[:, t, :], bno, -1.0, float(BUCKETS), ALU.mult, ALU.add))
                do(dve.tensor_copy(slotp, slot_no[:, :]))
                do(dve.tensor_copy(bcmp, bno))
                wait()
                if i == 0:
                    dve.sem_inc(m["g_free"], 1)
                dve.wait_ge(s2["moe_small_in"], 64 * i + 64)
                dve.wait_ge(m["logits_ps"], i + 1)
                do(dve.tensor_tensor(lg[:, :, :], B(4)[:, 0:128].rearrange("p (t n) -> p t n", t=TT)[:, :, 0:36], spread(brow, 1, TT), ALU.add))
                wait()
                top = rsm[:, 0:2]
                do(dve.tensor_reduce(top, lg[:, :, 0:4], AX_X, ALU.max))
                wait()
                dve.tensor_tensor(fx[:, :, 0:4], lg[:, :, 0:4], spread(top, 2, 4), ALU.subtract).then_inc(m["exp_in"], 1)
                first_hot(fm[:, :, 0:4], lg[:, :, 0:4], top, 4, m)
                do(dve.tensor_scalar(fm[:, :, 0:4], fm[:, :, 0:4], -1.0, -NEG, ALU.add, ALU.mult))
                wait()
                for t in range(TT):
                    do(dve.tensor_tensor(fk[:, t, :].rearrange("p (g e) -> p g e", g=4), lg[:, t, 4:36].rearrange("p (g e) -> p g e", g=4),
                                         spread(fm[:, t, 0:4], 2, EPG), ALU.add))
                wait()
                do(dve.tensor_copy(fm[:, :, :], fk[:, :, :]))
                wait()
                v1, v2 = rsm[:, 2:4], rsm[:, 4:6]
                do(dve.tensor_reduce(v1, fm[:, :, :], AX_X, ALU.max))
                wait()
                first_hot(oh1[:, :, :], fm[:, :, :], v1, NE, m)
                do(dve.scalar_tensor_tensor(fl(fm), fl(oh1), NEG, fl(fm), ALU.mult, ALU.add))
                wait()
                do(dve.tensor_reduce(v2, fm[:, :, :], AX_X, ALU.max))
                wait()
                first_hot(oh2[:, :, :], fm[:, :, :], v2, NE, m)
                dve.tensor_tensor(rsm[:, 8:10], v2, v1, ALU.subtract).then_inc(m["exp_in"], 1)
                do(dve.tensor_tensor(sel_e[:, :, :], oh1[:, :, :], oh2[:, :, :], ALU.add))
                wait()
                dve.sem_inc(m["sel_ready"], 1)
                dve.wait_ge(m["exp_out"], 2 * i + 2)
                do(dve.tensor_reduce(rsm[:, 6:8], fx[:, :, 0:4], AX_X, ALU.add))
                do(dve.tensor_scalar(rsm[:, 10:12], rsm[:, 8:10], 1.0, None, ALU.add))
                wait()
                do(dve.tensor_tensor(rsm[:, 12:14], rsm[:, 6:8], rsm[:, 10:12], ALU.mult))
                wait()
                do(dve.reciprocal(rsm[:, 14:16], rsm[:, 12:14]))
                wait()
                do(dve.tensor_tensor(rsm[:, 16:18], rsm[:, 14:16], rsm[:, 8:10], ALU.mult))
                wait()
                do(dve.tensor_tensor(oh1[:, :, :], oh1[:, :, :], spread(rsm[:, 14:16], 2, NE), ALU.mult))
                do(dve.tensor_tensor(oh2[:, :, :], oh2[:, :, :], spread(rsm[:, 16:18], 2, NE), ALU.mult))
                wait()
                do(dve.tensor_tensor(gg[:, :, :], oh1[:, :, :], oh2[:, :, :], ALU.add))
                dve.wait_ge(m["rank_ps"], i + 1)
                do(dve.scalar_tensor_tensor(fk[:, :, :], B(5)[:, 0:2 * NE].rearrange("p (t n) -> p t n", t=TT), 1.0, sel_e[:, :, :], ALU.add, ALU.mult))
                do(dve.tensor_reduce(passes_f[:, 0:1], B(5)[:, 2 * NE:3 * NE], AX_X, ALU.max))
                wait()
                do(dve.tensor_scalar(rk[:, :, :], fk[:, :, :], -1.0, None, ALU.add))
                for k in range(1, 4):
                    do(dve.tensor_scalar(passes_f[:, k:k + 1], passes_f[:, 0:1], float(SLOTS * k), None, ALU.is_gt))
                wait()
                do(dve.tensor_reduce(passes_f[:, 4:5], passes_f[:, 1:4], AX_X, ALU.add))
                wait()
                dve.tensor_scalar(passes_i[i][:, :], passes_f[0:1, 4:5], 1.0, None, ALU.add).then_inc(m["passes_ready"], 1)
                dve.wait_ge(m["passes_ready"], i + 1)
                n = dve.value_load(passes_i[i][0:1, 0:1], min_val=1, max_val=4)
                X, T, G, U = B(4), B(5), B(6), B(7)

                with dve.Fori(0, n) as q:
                    with dve.Fori(0, PAIRS) as pr:
                        it = (q + before) * PAIRS + pr
                        mo.start(it * MCHAIN + 2 * (q + before))
                        dve.wait_ge(m["gathered"], 2 * it + 2)
                        dve.wait_ge(m["pg_filled"], it + 1)
                        for t in range(TT):
                            for e in range(2):
                                c = slice(SLOTS * e, SLOTS * e + SLOTS)
                                r1 = rk[:, t, bass.ds(2 * pr + e, 1)]
                                g1 = gg[:, t, bass.ds(2 * pr + e, 1)]
                                mo.do(dve.tensor_scalar(pickg[:, t, c], slotp, r1, g1, ALU.is_equal, ALU.mult))
                                mo.do(dve.tensor_scalar(pick[:, t, c], slotp, r1, None, ALU.is_equal))
                        mo.wait()
                        dve.sem_inc(m["p_ready"], 1)

                        def bias_of(bk):
                            if with_bias:
                                mo.do(dve.tensor_scalar(mask_b, bkt, bcmp[:, bass.ds(bk, 1)], None, ALU.is_equal))
                                mo.wait()
                                for h in range(12):
                                    mo.do(dve.scalar_tensor_tensor(fl(bias[:, h]), mask_b, rbt[:, bass.ds(12 * bk + h, 1)], fl(bias[:, h]),
                                                                   ALU.mult, ALU.add))

                        bias_of(2 * pr)
                        dve.wait_ge(m["xt_filled"], 2 * it + 1)
                        mo.do(dve.tensor_tensor(xeT[:, 0:4, :], X.rearrange("p (d n) -> p d n", d=4), spread(gm[:, 2 * i + 1, 0:4], 2, P), ALU.mult))
                        mo.wait()
                        dve.tensor_tensor(xeT[:, 0:4, :], xeT[:, 0:4, :], spread(modc[:, i, 24:28], 2, P), ALU.add).then_inc(m["xt_drained_v"], 1)
                        bias_of(2 * pr + 1)
                        dve.wait_ge(m["tanh_done"], it + 1)
                        dve.scalar_tensor_tensor(zz, th, 1.0, G, ALU.add, ALU.mult).then_inc(m["g_free"], 1)
                        mo.wait()
                        dve.wait_ge(m["g_free"], it + 2)
                        dve.wait_ge(m["u_filled"], it + 2)
                        dve.scalar_tensor_tensor(aa, zz, 0.5, U, ALU.mult, ALU.mult).then_inc(m["a_ready"], 1)
                        dve.wait_ge(m["at_filled"], it + 1)
                        dve.tensor_copy(aTe[:, :, :], T.rearrange("p (k n) -> p k n", k=4)).then_inc(m["at_drained"], 1)
                        mo.wait()
                        dve.sem_inc(m["own_loop"], MCHAIN - mo.n)
                    mo.start((q + before) * (PAIRS * MCHAIN + 2) + PAIRS * MCHAIN)
                    mo.do(dve.tensor_scalar(slotp, slotp, float(SLOTS), None, ALU.add))
                    mo.do(dve.tensor_scalar(bcmp, bcmp, 1000.0, None, ALU.add))
                    mo.wait()
                dve.wait_ge(m["scattered"], PAIRS * (n + before) + i + 1)
                dve.wait_ge(s2["gate_row_drained"], i + 1)
                residual(2 * i + 2, [region(0, 1024), region(1024, 1024)])
                dve.sem_inc(m["acc_done"], 1)
                return n

            n0 = moe(0, True, 0)
            norm_x2()
            diag(dg_m, 1, 16)
            drained("ki")
            for h in range(8):
                drained("rel%d" % h)
                for t in range(TT):
                    src, w = sc4[:, h % 4, S * t:S * t + S], wix[:, t, h:h + 1]
                    if h == 0:
                        ins = dve.tensor_scalar(isc[:, t, :], src, w, None, ALU.mult)
                    else:
                        ins = dve.scalar_tensor_tensor(isc[:, t, :], src, w, isc[:, t, :], ALU.mult, ALU.add)
                    if t == 0:
                        do(ins)
                wait()
                ins.then_inc(s2["rel_used"], 1)
                dve.wait_ge(s2["rel_used"], h + 1)
            do(dve.scalar_tensor_tensor(fl(isc), fl(isc), (32 * 8) ** -0.5, fl(cmask), ALU.mult, ALU.add))
            wait()
            for r in range(TOPK // 8):
                for t in range(TT):
                    do(dve.max(top8[:, t, :], isc[:, t, :]))
                wait()
                for t in range(TT):
                    do(dve.match_replace(isc[:, t, :], top8[:, t, :], isc[:, t, :], -3e38))
                wait()
            do(dve.tensor_scalar(fl(iwk), fl(isc), -2e38, NEG, ALU.is_gt, ALU.mult))
            dve.wait_ge(s2["lam_exp"], 1)
            do(dve.scalar_tensor_tensor(lam[:, 2:3], lam[:, 0:1], -1.0, lam[:, 1:2], ALU.mult, ALU.add))
            wait()
            do(dve.tensor_scalar(lam[:, 2:3], lam[:, 2:3], -LAMBDA_INIT, None, ALU.add))
            for g in range(4):
                for i, heads in enumerate(FULL):
                    h0, t = heads[0][0], heads[0][1]
                    dve.wait_ge(s2["scores"], 4 * g + i + 1)
                    if g > 0:
                        dve.wait_ge(s2["pt_filled"], 4 * g)
                    dst = sc4[:, i, :].rearrange("p (h n) -> p h n", h=2)
                    hb = (4 * g if g < 2 else 8) + h0
                    do(dve.scalar_tensor_tensor(dst, B(4 + i).rearrange("p (h n) -> p h n", h=2), 64 ** -0.5, bias[:, hb:hb + 2, t, :], ALU.mult, ALU.add))
                    wait()
                    if g < 2:
                        do(dve.tensor_tensor(dst, dst, spread(iwk[:, t, :], 1, 2), ALU.add))
                        wait()
                    dve.tensor_reduce(nmx[:, i, 0:2], dst, AX_X, ALU.max, negate=True).then_inc(s2["masked"], 1)
                dve.wait_ge(s2["exp_done"], 4 * g + 4)
                do(dve.reciprocal(rsum[:, :, :], esum[:, :, :]))
                wait()
                if g < 2:
                    drained("oc%d" % g)
                    v = heads_of(xn, 256 * g, 4, 64)
                    do(dve.tensor_tensor(v, v, spread(rsum[:, :, :], 3, 64), ALU.mult))
                else:
                    drained("od%d1" % (g - 2))
                    v = heads_of(xn, 512, 4, 128) if g == 2 else od2.rearrange("p t (h d) -> p t h d", h=4)
                    do(dve.tensor_tensor(v, v, spread(rsum[:, :, :], 3, 128), ALU.mult))
            wait()
            do(dve.scalar_tensor_tensor(xn[:, :, 512:1024], od2, lam[:, 2:3], xn[:, :, 512:1024], ALU.mult, ALU.add))
            wait()
            v = heads_of(xn, 512, 4, 128)
            sq = region(0, 1024).rearrange("p (t h d) -> p t h d", t=TT, h=4)
            do(dve.tensor_tensor(sq, v, v, ALU.mult))
            wait()
            r = stat_out(dve.tensor_reduce(stat_col()[:, 0:8], sq, AX_X, ALU.add))
            per_group(v, v, r, 4, 128).then_inc(s2["lam_ready"], 1)
            dve.wait_ge(s2["out_filled"], 4)
            drained("gate1b")
            residual(3, [region(0, 1024), region(1024, 1024)])
            moe(1, False, n0)
            norm_x2()
            dve.wait_ge(s2["final_in"], 16)
            dve.wait_ge(s2["xn_ready"], 2 * 5)
            for t in range(TT):
                ins = dve.tensor_tensor(xn[:, t, :], xn[:, t, :], fin_g, ALU.mult)
                if t == 0:
                    do(ins)
            wait()
            ins.then_inc(s2["o_ready"], 1)


INPUTS = ["x", "positions", "w_in", "conv_w", "conv_b", "b_igate", "b_fgate", "g_mix_norm", "g_mlstm_out", "g_moba_q", "g_moba_k",
          "g_moba_out", "g_cq", "g_ckv", "w_uq", "w_ukv", "g_mla_q", "g_mla_k", "g_mla_out", "w_out", "g_mlp_norm", "w_up", "w_down",
          "c_2", "positions_2", "rel_bias_2", "norm_g_2", "final_norm_g_2", "ada_w_2", "ada_b_2", "ab_w_in_2", "ab_conv_a_2",
          "ab_conv_b_2", "ab_conv_b_bias_2", "ab_ln_g_2", "ab_ln_b_2", "ab_w_out_2", "cd_w_in_2", "diff_lam_2", "diff_norm_g_2",
          "cd_w_out_2", "moe_wr_g_2", "moe_br_g_2", "moe_wr_e_2", "moe_br_e_2", "moe_w_gate_2", "moe_w_up_2", "moe_w_down_2"]


def kernel(**inputs):
    from concourse import bacc
    from concourse.bass_utils import run_bass_kernel_spmd

    nc = bacc.Bacc("TRN2", target_bir_lowering=False, num_devices=1)
    arrays, aps = {}, {}
    for name in INPUTS:
        array = np.ascontiguousarray(inputs[name])
        arrays[f"in_{name}"] = array
        aps[name] = nc.dram_tensor(f"in_{name}", array.shape, mybir.dt.from_np(array.dtype), kind="ExternalInput").ap()
    out = nc.dram_tensor("out", (1, S, D), F32, kind="ExternalOutput").ap()
    first_and_second_block(nc, aps, out)
    result = run_bass_kernel_spmd(nc, [arrays], core_ids=[0])
    return result.results[0]["out"]
```
